# Optimizing a Trainium2 kernel written in Bass

```python
import jax
import jax.numpy as jnp
from jax import lax
import numpy as np
import math

D_MODEL = 1024
BATCH = 1
SEQ = 512
DEPTH = 2

GRID_W = 64
CTX_LEN = 256
CHUNK = 64
GLA_HEADS = 4
GLA_DK = 64
GLA_DV = 128
GLA_GATE_RANK = 16
GLA_GATE_TAU = 16.0
ATT_Q_HEADS = 8
ATT_KV_HEADS = 2
ATT_HEAD_DIM = 64
ATT_GROUP = ATT_Q_HEADS // ATT_KV_HEADS
ROPE_AXIS_DIM = ATT_HEAD_DIM // 2
ROPE_THETA = 10000.0
Q_BLOCK = 128
HGRN_HEADS = 8
HGRN_DF = 128
HGRN_DV = D_MODEL // HGRN_HEADS
D_FF = ((8 * D_MODEL + 3 * 256 - 1) // (3 * 256)) * 256

EVEN_SIZES = (GLA_HEADS * GLA_DK, GLA_HEADS * GLA_DK, GLA_HEADS * GLA_DV, GLA_HEADS * GLA_DV, 2 * GLA_GATE_RANK,
              ATT_Q_HEADS * ATT_HEAD_DIM, ATT_KV_HEADS * ATT_HEAD_DIM, ATT_KV_HEADS * ATT_HEAD_DIM)
ODD_SIZES = (HGRN_HEADS * HGRN_DF,) * 3 + (HGRN_HEADS * HGRN_DV,) * 2
EVEN_MIX = GLA_HEADS * GLA_DV + ATT_Q_HEADS * ATT_HEAD_DIM
ODD_MIX = HGRN_HEADS * HGRN_DV


def _rms(x, gain, eps=1e-6):
    xf = x.astype(jnp.float32)
    y = xf * lax.rsqrt(jnp.mean(xf * xf, axis=-1, keepdims=True) + eps)
    return (y * gain.astype(jnp.float32)).astype(x.dtype)

def _modulate(h, shift, scale):
    return h * (1 + scale) + shift

def _split(a, sizes):
    return jnp.split(a, np.cumsum(sizes)[:-1].tolist(), axis=-1)

def _heads(a, n_heads):
    B, N, _ = a.shape
    return a.reshape(B, N, n_heads, -1).transpose(0, 2, 1, 3)

def _merge(a):
    B, H, N, d = a.shape
    return a.transpose(0, 2, 1, 3).reshape(B, N, H * d)

def _gated_readout(o, og, gain):
    return _merge(_rms(o, gain) * jax.nn.silu(og))

def _swiglu(h, w_gate, w_up, w_down):
    return (jax.nn.silu(h @ w_gate) * (h @ w_up)) @ w_down

def _chunk_gla(q, k, v, g, s0):
    B, H, T, K = q.shape
    V = v.shape[-1]
    n = T // CHUNK

    def blocks(a):
        return jnp.moveaxis(a.astype(jnp.float32).reshape(B, H, n, CHUNK, a.shape[-1]), 2, 0)

    tri = jnp.tril(jnp.ones((CHUNK, CHUNK), dtype=bool))[:, :, None]

    def step(s, blk):
        qc, kc, vc, gc = blk
        G = jnp.cumsum(gc, axis=2)
        decay = jnp.exp(jnp.where(tri, G[:, :, :, None, :] - G[:, :, None, :, :], -jnp.inf))
        scores = jnp.einsum('bhik,bhjk,bhijk->bhij', qc, kc, decay)
        o = jnp.einsum('bhij,bhjv->bhiv', scores, vc) + jnp.einsum('bhik,bhkv->bhiv', qc * jnp.exp(G), s)
        G_last = G[:, :, -1:, :]
        s = s * jnp.exp(G_last)[:, :, 0, :, None] + jnp.einsum('bhjk,bhjv->bhkv', kc * jnp.exp(G_last - G), vc)
        return s, o

    s, o = lax.scan(step, s0, (blocks(q), blocks(k), blocks(v), blocks(g)))
    return jnp.moveaxis(o, 0, 2).reshape(B, H, T, V).astype(v.dtype), s

def _directional_scan(q, k, v, g, n_ctx, reverse):
    def seg(a, sl):
        a = a[:, :, sl]
        return jnp.flip(a, 2) if reverse else a
    c_sl, t_sl = slice(0, n_ctx), slice(n_ctx, None)
    B, H, _, K = q.shape
    s0 = jnp.zeros((B, H, K, v.shape[-1]), jnp.float32)
    o_ctx, s_ctx = _chunk_gla(seg(q, c_sl), seg(k, c_sl), seg(v, c_sl), seg(g, c_sl), s0)
    o_lat, _ = _chunk_gla(seg(q, t_sl), seg(k, t_sl), seg(v, t_sl), seg(g, t_sl), s_ctx)
    if reverse:
        o_ctx, o_lat = jnp.flip(o_ctx, 2), jnp.flip(o_lat, 2)
    return o_ctx, o_lat

def _axial_rope_tables(n_tokens):
    rows_n = n_tokens // GRID_W
    row = jnp.repeat(jnp.arange(rows_n), GRID_W).astype(jnp.float32)
    col = jnp.tile(jnp.arange(GRID_W), rows_n).astype(jnp.float32)
    inv = ROPE_THETA ** (-jnp.arange(0, ROPE_AXIS_DIM, 2, dtype=jnp.float32) / ROPE_AXIS_DIM)
    ang = jnp.concatenate([row[:, None] * inv, col[:, None] * inv], axis=-1)
    return jnp.cos(ang), jnp.sin(ang)

def _rope(x, cos, sin):
    xf = x.astype(jnp.float32).reshape(x.shape[:-1] + (-1, 2))
    x0, x1 = xf[..., 0], xf[..., 1]
    out = jnp.stack([x0 * cos - x1 * sin, x0 * sin + x1 * cos], axis=-1)
    return out.reshape(x.shape).astype(x.dtype)

def _softmax_attend(q, k, v):
    s = jnp.einsum('bhgqd,bhkd->bhgqk', q, k, preferred_element_type=jnp.float32) * (ATT_HEAD_DIM ** -0.5)
    p = jax.nn.softmax(s, axis=-1).astype(v.dtype)
    return jnp.einsum('bhgqk,bhkd->bhgqd', p, v)

def _even_mixer(h_ctx, h_lat, w_in, gla_w_gate, gla_b_gate, gla_out_norm, att_q_norm, att_k_norm, cos, sin, ctx_out):
    B, n_ctx, _ = h_ctx.shape
    h = jnp.concatenate([h_ctx, h_lat], axis=1)
    N = h.shape[1]
    T = N - n_ctx
    gq, gk, gv, gog, gz, aq, ak, av = _split(h @ w_in, EVEN_SIZES)

    q = _heads(gq, GLA_HEADS) * (GLA_DK ** -0.5)
    k = _heads(gk, GLA_HEADS)
    v = _heads(gv, GLA_HEADS)
    og = _heads(gog, GLA_HEADS)
    dirs = []
    for d, z in enumerate(jnp.split(gz, 2, axis=-1)):
        logit = (z @ gla_w_gate[d] + gla_b_gate[d]).astype(jnp.float32)
        g = _heads(jax.nn.log_sigmoid(logit) / GLA_GATE_TAU, GLA_HEADS)
        dirs.append(_directional_scan(q, k, v, g, n_ctx, reverse=(d == 1)))
    a_lat = _gated_readout(dirs[0][1] + dirs[1][1], og[:, :, n_ctx:], gla_out_norm)

    qa = _rms(aq.reshape(B, N, ATT_KV_HEADS, ATT_GROUP, ATT_HEAD_DIM), att_q_norm).transpose(0, 2, 3, 1, 4)
    ka = _rms(ak.reshape(B, N, ATT_KV_HEADS, ATT_HEAD_DIM), att_k_norm).transpose(0, 2, 1, 3)
    va = av.reshape(B, N, ATT_KV_HEADS, ATT_HEAD_DIM).transpose(0, 2, 1, 3)
    q_lat = _rope(qa[:, :, :, n_ctx:], cos, sin)
    k_all = jnp.concatenate([ka[:, :, :n_ctx], _rope(ka[:, :, n_ctx:], cos, sin)], axis=2)
    q_blocks = jnp.moveaxis(q_lat.reshape(B, ATT_KV_HEADS, ATT_GROUP, T // Q_BLOCK, Q_BLOCK, ATT_HEAD_DIM), 3, 0)
    o_blocks = lax.map(lambda qb: _softmax_attend(qb, k_all, va), q_blocks)
    b_lat = jnp.moveaxis(o_blocks, 0, 3).reshape(B, ATT_KV_HEADS, ATT_GROUP, T, ATT_HEAD_DIM)
    b_lat = b_lat.transpose(0, 3, 1, 2, 4).reshape(B, T, ATT_Q_HEADS * ATT_HEAD_DIM)
    o_lat = jnp.concatenate([a_lat, b_lat], axis=-1)
    if not ctx_out:
        return None, o_lat
    a_ctx = _gated_readout(dirs[0][0] + dirs[1][0], og[:, :, :n_ctx], gla_out_norm)
    b_ctx = _softmax_attend(qa[:, :, :, :n_ctx], ka[:, :, :n_ctx], va[:, :, :n_ctx])
    b_ctx = b_ctx.transpose(0, 3, 1, 2, 4).reshape(B, n_ctx, ATT_Q_HEADS * ATT_HEAD_DIM)
    return jnp.concatenate([a_ctx, b_ctx], axis=-1), o_lat

def _odd_mixer(h_ctx, h_lat, w_in, lower_bounds, layer, out_norm, ctx_out):
    n_ctx = h_ctx.shape[1]
    h = jnp.concatenate([h_ctx, h_lat], axis=1)
    fq, f_fwd, f_bwd, fi, fog = _split(h @ w_in, ODD_SIZES)
    q = _heads(jax.nn.silu(fq), HGRN_HEADS)
    i = _heads(fi, HGRN_HEADS)
    og = _heads(fog, HGRN_HEADS)
    lbs = jnp.cumsum(jax.nn.softmax(lower_bounds.astype(jnp.float32), axis=1), axis=1)
    lb = (lbs[:, layer] - lbs[:, 0]).reshape(2, HGRN_HEADS, 1, HGRN_DF)
    dirs = []
    for d, f in enumerate((f_fwd, f_bwd)):
        log_f = jnp.logaddexp(jnp.log(lb[d]), jnp.log1p(-lb[d]) + jax.nn.log_sigmoid(_heads(f, HGRN_HEADS).astype(jnp.float32)))
        k = -jnp.expm1(log_f)
        dirs.append(_directional_scan(q, k, i, log_f, n_ctx, reverse=(d == 1)))
    o_lat = _gated_readout(dirs[0][1] + dirs[1][1], og[:, :, n_ctx:], out_norm)
    if not ctx_out:
        return None, o_lat
    return _gated_readout(dirs[0][0] + dirs[1][0], og[:, :, :n_ctx], out_norm), o_lat

def first_inputs(seed: int = 0) -> dict:
    key = jax.random.key(seed)
    ks = iter(jax.random.split(key, 32))
    n_even, n_odd = (DEPTH + 1) // 2, DEPTH // 2
    D = D_MODEL

    def nrm(shape, scale):
        return scale * jax.random.normal(next(ks), shape, jnp.float32)

    def gain(shape):
        return 1.0 + nrm(shape, 0.02)

    return {
        'x': nrm((BATCH, SEQ, D), 1.0),
        'c': nrm((BATCH, D), 1.0),
        'ctx': nrm((BATCH, CTX_LEN, D), 1.0),
        'c_ctx': nrm((D,), 1.0),
        'mod_w': nrm((DEPTH, D, 6 * D), D ** -0.5),
        'mod_b': nrm((DEPTH, 6 * D), 0.02),
        'norm_pre_mix': gain((DEPTH, D)),
        'norm_post_mix': gain((DEPTH, D)),
        'norm_pre_ffn': gain((DEPTH, D)),
        'norm_post_ffn': gain((DEPTH, D)),
        'even_w_in': nrm((n_even, D, sum(EVEN_SIZES)), D ** -0.5),
        'gla_w_gate': nrm((n_even, 2, GLA_GATE_RANK, GLA_HEADS * GLA_DK), GLA_GATE_RANK ** -0.5),
        'gla_b_gate': nrm((n_even, 2, GLA_HEADS * GLA_DK), 0.02),
        'gla_out_norm': gain((n_even, GLA_DV)),
        'att_q_norm': gain((n_even, ATT_HEAD_DIM)),
        'att_k_norm': gain((n_even, ATT_HEAD_DIM)),
        'even_w_out': nrm((n_even, EVEN_MIX, D), EVEN_MIX ** -0.5),
        'odd_w_in': nrm((n_odd, D, sum(ODD_SIZES)), D ** -0.5),
        'hgrn_lower_bounds': nrm((2, DEPTH, HGRN_HEADS * HGRN_DF), 0.1),
        'hgrn_out_norm': gain((n_odd, HGRN_DV)),
        'odd_w_out': nrm((n_odd, ODD_MIX, D), ODD_MIX ** -0.5),
        'ffn_w_gate': nrm((DEPTH, D, D_FF), D ** -0.5),
        'ffn_w_up': nrm((DEPTH, D, D_FF), D ** -0.5),
        'ffn_w_down': nrm((DEPTH, D_FF, D), D_FF ** -0.5),
    }

def first_block(x, c, ctx, c_ctx, mod_w, mod_b, norm_pre_mix, norm_post_mix, norm_pre_ffn, norm_post_ffn,
              even_w_in, gla_w_gate, gla_b_gate, gla_out_norm, att_q_norm, att_k_norm, even_w_out,
              odd_w_in, hgrn_lower_bounds, hgrn_out_norm, odd_w_out, ffn_w_gate, ffn_w_up, ffn_w_down):
    cos, sin = _axial_rope_tables(x.shape[1])
    sc = jax.nn.silu(c)
    scc = jax.nn.silu(c_ctx)
    x_ctx, x_lat = ctx, x
    for l in range(DEPTH):
        last = l == DEPTH - 1
        j = l // 2
        m_lat = jnp.split((sc @ mod_w[l] + mod_b[l])[:, None, :], 6, axis=-1)
        m_ctx = jnp.split((scc @ mod_w[l] + mod_b[l])[None, None, :], 6, axis=-1)
        h_ctx = _modulate(_rms(x_ctx, norm_pre_mix[l]), m_ctx[0], m_ctx[1])
        h_lat = _modulate(_rms(x_lat, norm_pre_mix[l]), m_lat[0], m_lat[1])
        if l % 2 == 0:
            o_ctx, o_lat = _even_mixer(h_ctx, h_lat, even_w_in[j], gla_w_gate[j], gla_b_gate[j], gla_out_norm[j],
                                       att_q_norm[j], att_k_norm[j], cos, sin, not last)
            w_out = even_w_out[j]
        else:
            o_ctx, o_lat = _odd_mixer(h_ctx, h_lat, odd_w_in[j], hgrn_lower_bounds, l, hgrn_out_norm[j], not last)
            w_out = odd_w_out[j]
        x_lat = x_lat + m_lat[2] * _rms(o_lat @ w_out, norm_post_mix[l])
        h_lat = _modulate(_rms(x_lat, norm_pre_ffn[l]), m_lat[3], m_lat[4])
        x_lat = x_lat + m_lat[5] * _rms(_swiglu(h_lat, ffn_w_gate[l], ffn_w_up[l], ffn_w_down[l]), norm_post_ffn[l])
        if not last:
            x_ctx = x_ctx + m_ctx[2] * _rms(o_ctx @ w_out, norm_post_mix[l])
            h_ctx = _modulate(_rms(x_ctx, norm_pre_ffn[l]), m_ctx[3], m_ctx[4])
            x_ctx = x_ctx + m_ctx[5] * _rms(_swiglu(h_ctx, ffn_w_gate[l], ffn_w_up[l], ffn_w_down[l]), norm_post_ffn[l])
    return x_lat


DEPTH_2 = 1

N_BRANCHES = 2
EPS = 1e-6
F32 = jnp.float32

DN_HEADS = 8
DN_DK = 128
DN_DV = 128
DN_CONV = 5
DN_CHUNK = 64
MLA_HEADS = 8
MLA_Q_RANK = 384
MLA_KV_RANK = 256
MLA_NOPE = 128
MLA_ROPE = 64
MLA_QK_DIM = MLA_NOPE + MLA_ROPE
MLA_V = 128
ROPE_BASE = 10000.0
N_EXPERTS = 16
EC_CAPACITY = 2
EXPERT_FF = 1408

DN_QKV_DIM = 2 * DN_HEADS * DN_DK + DN_HEADS * DN_DV
OFF_Z = DN_QKV_DIM
OFF_ALPHA = OFF_Z + DN_HEADS * DN_DV
OFF_BETA = OFF_ALPHA + 2 * DN_HEADS
OFF_CQ = OFF_BETA + 2 * DN_HEADS
OFF_CKV = OFF_CQ + MLA_Q_RANK
OFF_KROPE = OFF_CKV + MLA_KV_RANK
OFF_GATE = OFF_KROPE + MLA_ROPE
D_IN = OFF_GATE + N_BRANCHES * D_MODEL
IN_OFFSETS = (OFF_Z, OFF_ALPHA, OFF_BETA, OFF_CQ, OFF_CKV, OFF_KROPE, OFF_GATE)


def rms_norm(x, g):
    xf = x.astype(F32)
    y = xf * lax.rsqrt(jnp.mean(xf * xf, axis=-1, keepdims=True) + EPS)
    return y.astype(x.dtype) * g

def l2_norm(x):
    return x * lax.rsqrt(jnp.sum(x * x, axis=-1, keepdims=True) + EPS)

def adaln(cond, ada_w, ada_b):
    mod = jax.nn.silu(cond) @ ada_w + ada_b
    return jnp.split(mod[:, None, :], 6, axis=-1)

def modulate(x, g, shift, scale):
    return rms_norm(x, g) * (1.0 + scale) + shift

def short_conv(x, w):
    pad = DN_CONV // 2
    y = lax.conv_general_dilated(x, w[:, None, :], window_strides=(1,), padding=[(pad, pad)],
                                 dimension_numbers=('NWC', 'WIO', 'NWC'), feature_group_count=x.shape[-1])
    return jax.nn.silu(y)

def gated_delta_chunked(q, k, v, g, beta, s0):
    b_, n_tok, n_h, dk = q.shape
    dv = v.shape[-1]
    n_chunk = n_tok // DN_CHUNK

    def to_chunks(t):
        return jnp.moveaxis(t.reshape(b_, n_chunk, DN_CHUNK, n_h, *t.shape[3:]), 3, 1)

    q, k, v, g, beta = (to_chunks(t) for t in (q, k, v, g, beta))
    q = q * dk ** -0.5
    g = jnp.cumsum(g, axis=-1)
    incl = jnp.tril(jnp.ones((DN_CHUNK, DN_CHUNK), dtype=bool))
    strict = jnp.tril(jnp.ones((DN_CHUNK, DN_CHUNK), dtype=bool), -1)
    decay = jnp.exp(jnp.where(incl, g[..., :, None] - g[..., None, :], -jnp.inf))
    k_beta = k * beta[..., None]
    m = jnp.where(strict, jnp.einsum('bhnid,bhnjd->bhnij', k_beta, k) * decay, 0.0)
    eye = jnp.eye(DN_CHUNK, dtype=q.dtype)
    t_inv = lax.linalg.triangular_solve(m + eye, jnp.broadcast_to(eye, m.shape), left_side=True,
                                        lower=True, unit_diagonal=True)
    u = jnp.einsum('bhnij,bhnjd->bhnid', t_inv, v * beta[..., None])
    w = jnp.einsum('bhnij,bhnjd->bhnid', t_inv, k_beta * jnp.exp(g)[..., None])
    qk = jnp.where(incl, jnp.einsum('bhnid,bhnjd->bhnij', q, k) * decay, 0.0)
    q_dec = q * jnp.exp(g)[..., None]
    k_dec = k * jnp.exp(g[..., -1:] - g)[..., None]
    chunk_decay = jnp.exp(g[..., -1])

    def chunk_step(s, xs):
        qk_c, q_c, k_c, u_c, w_c, a_c = xs
        v_new = u_c - jnp.einsum('bhik,bhkv->bhiv', w_c, s)
        o_c = jnp.einsum('bhik,bhkv->bhiv', q_c, s) + jnp.einsum('bhij,bhjv->bhiv', qk_c, v_new)
        s = s * a_c[..., None, None] + jnp.einsum('bhik,bhiv->bhkv', k_c, v_new)
        return s, o_c

    xs = tuple(jnp.moveaxis(t, 2, 0) for t in (qk, q_dec, k_dec, u, w, chunk_decay))
    s_final, o = lax.scan(chunk_step, s0, xs)
    o = jnp.transpose(o, (1, 0, 3, 2, 4)).reshape(b_, n_tok, n_h, dv)
    return o, s_final

def deltanet_inputs(qkv, alpha, beta_logit, conv_w, a_log, dt_bias):
    b_, n_tok, _ = qkv.shape
    qkv = short_conv(qkv, conv_w)
    q, k, v = jnp.split(qkv, [DN_HEADS * DN_DK, 2 * DN_HEADS * DN_DK], axis=-1)
    q = l2_norm(q.astype(F32).reshape(b_, n_tok, DN_HEADS, DN_DK))
    k = l2_norm(k.astype(F32).reshape(b_, n_tok, DN_HEADS, DN_DK))
    v = v.astype(F32).reshape(b_, n_tok, DN_HEADS, DN_DV)
    alpha = alpha.astype(F32).reshape(b_, n_tok, 2, DN_HEADS)
    g = -jnp.exp(a_log.astype(F32)) * jax.nn.softplus(alpha + dt_bias.astype(F32))
    beta = jax.nn.sigmoid(beta_logit.astype(F32).reshape(b_, n_tok, 2, DN_HEADS))
    return q, k, v, g, beta

def deltanet_bidir(q, k, v, g, beta, s0_fwd, s0_bwd):
    o_f, s_f = gated_delta_chunked(q, k, v, g[:, :, 0], beta[:, :, 0], s0_fwd)
    flip = lambda t: jnp.flip(t, axis=1)
    o_b, s_b = gated_delta_chunked(flip(q), flip(k), flip(v), flip(g[:, :, 1]), flip(beta[:, :, 1]), s0_bwd)
    return o_f + flip(o_b), s_f, s_b

def deltanet_out(o, z, norm_g):
    b_, n_tok = o.shape[:2]
    zf = z.astype(F32).reshape(b_, n_tok, DN_HEADS, DN_DV)
    y = rms_norm(o, norm_g.astype(F32)) * jax.nn.silu(zf)
    return y.reshape(b_, n_tok, DN_HEADS * DN_DV).astype(z.dtype)

def axial_rope_tables(rows, dtype):
    row = jnp.repeat(jnp.arange(rows), GRID_W).astype(F32)
    col = jnp.broadcast_to(jnp.arange(GRID_W), (rows, GRID_W)).reshape(-1).astype(F32)
    n_freq = MLA_ROPE // 4
    inv_freq = ROPE_BASE ** (-jnp.arange(n_freq, dtype=F32) / n_freq)
    ang_r = row[:, None] * inv_freq
    ang_c = col[:, None] * inv_freq
    ang = jnp.concatenate([ang_r, ang_r, ang_c, ang_c], axis=-1)[:, None, :]
    return jnp.cos(ang).astype(dtype), jnp.sin(ang).astype(dtype)

def apply_rope_tail(t, rope):
    cos, sin = rope
    nope, pe = jnp.split(t, [MLA_NOPE], axis=-1)
    x1, x2, x3, x4 = jnp.split(pe, 4, axis=-1)
    rot = jnp.concatenate([-x2, x1, -x4, x3], axis=-1)
    return jnp.concatenate([nope, pe * cos + rot * sin], axis=-1)

def mla_queries(c_q, q_a_norm_g, w_uq, q_norm_g, rope):
    b_, n_tok, _ = c_q.shape
    q = (rms_norm(c_q, q_a_norm_g) @ w_uq).reshape(b_, n_tok, MLA_HEADS, MLA_QK_DIM)
    q = rms_norm(q, q_norm_g)
    if rope is not None:
        q = apply_rope_tail(q, rope)
    return jnp.transpose(q, (0, 2, 1, 3))

def mla_keys_values(c_kv, k_rope, kv_a_norm_g, w_ukv, k_norm_g, rope):
    b_, n_tok, _ = c_kv.shape
    kv = (rms_norm(c_kv, kv_a_norm_g) @ w_ukv).reshape(b_, n_tok, MLA_HEADS, MLA_NOPE + MLA_V)
    k_nope, v = jnp.split(kv, [MLA_NOPE], axis=-1)
    k_pe = jnp.broadcast_to(k_rope[:, :, None, :], (b_, n_tok, MLA_HEADS, MLA_ROPE))
    k = rms_norm(jnp.concatenate([k_nope, k_pe], axis=-1), k_norm_g)
    if rope is not None:
        k = apply_rope_tail(k, rope)
    return jnp.transpose(k, (0, 2, 1, 3)), jnp.transpose(v, (0, 2, 1, 3))

def softmax_attention(q, k, v):
    b_, n_h, n_tok, dh = q.shape
    n_blk = n_tok // Q_BLOCK
    q_blocks = jnp.moveaxis(q.reshape(b_, n_h, n_blk, Q_BLOCK, dh), 2, 0)
    scale = dh ** -0.5

    def attend_block(qb):
        s = jnp.einsum('bhqd,bhkd->bhqk', qb, k, preferred_element_type=F32) * scale
        p = jax.nn.softmax(s, axis=-1).astype(v.dtype)
        return jnp.einsum('bhqk,bhkd->bhqd', p, v)

    o = lax.map(attend_block, q_blocks)
    o = jnp.moveaxis(o, 0, 2).reshape(b_, n_h, n_tok, -1)
    return jnp.transpose(o, (0, 2, 1, 3)).reshape(b_, n_tok, -1)

def merge_branches(y_a, y_b, gate_logits, w_out_a, w_out_b, w_o):
    g_a, g_b = jnp.split(jax.nn.sigmoid(gate_logits), N_BRANCHES, axis=-1)
    return (g_a * (y_a @ w_out_a) + g_b * (y_b @ w_out_b)) @ w_o

def expert_choice_moe(h, router_w, w_gate, w_up, w_down):
    b_, n_tok, d = h.shape
    cap = EC_CAPACITY * n_tok // N_EXPERTS
    affinity = jax.nn.softmax((h @ router_w).astype(F32), axis=-1)
    gate, idx = lax.top_k(jnp.swapaxes(affinity, 1, 2), cap)
    xe = jax.vmap(lambda hb, ib: hb[ib])(h, idx)
    hid = jax.nn.silu(jnp.einsum('becd,edf->becf', xe, w_gate)) * jnp.einsum('becd,edf->becf', xe, w_up)
    ye = jnp.einsum('becf,efd->becd', hid, w_down) * gate[..., None].astype(h.dtype)
    return jax.vmap(lambda ib, yb: jnp.zeros((n_tok, d), yb.dtype).at[ib.reshape(-1)].add(yb.reshape(-1, d)))(idx, ye)

def second_inputs(seed: int = 0) -> dict:
    key = jax.random.key(seed)
    ks = jax.random.split(key, 26)
    d = D_MODEL
    nrm = lambda k, shape, scale: jax.random.normal(k, shape, F32) * scale
    gain = lambda k, n: 1.0 + 0.02 * jax.random.normal(k, (DEPTH_2, n), F32)
    dt = jnp.exp(jax.random.uniform(ks[10], (DEPTH_2, 2, DN_HEADS), F32, math.log(1e-3), math.log(1e-1)))
    return {
        'x': nrm(ks[0], (BATCH, SEQ, d), 1.0),
        'c': nrm(ks[1], (BATCH, d), 1.0),
        'ctx': nrm(ks[2], (BATCH, CTX_LEN, d), 1.0),
        'c_ctx': nrm(ks[3], (d,), 1.0),
        'ada_w': nrm(ks[4], (DEPTH_2, d, 6 * d), d ** -0.5),
        'ada_b': nrm(ks[5], (DEPTH_2, 6 * d), 0.02),
        'norm1_g': gain(ks[6], d),
        'norm2_g': gain(ks[7], d),
        'w_in': nrm(ks[8], (DEPTH_2, d, D_IN), d ** -0.5),
        'conv_w': nrm(ks[9], (DEPTH_2, DN_CONV, DN_QKV_DIM), DN_CONV ** -0.5),
        'a_log': jnp.log(jax.random.uniform(ks[11], (DEPTH_2, 2, DN_HEADS), F32, 1.0, 16.0)),
        'dt_bias': dt + jnp.log(-jnp.expm1(-dt)),
        'dn_norm_g': gain(ks[12], DN_DV),
        'w_out_a': nrm(ks[13], (DEPTH_2, DN_HEADS * DN_DV, d), (DN_HEADS * DN_DV) ** -0.5),
        'q_a_norm_g': gain(ks[14], MLA_Q_RANK),
        'w_uq': nrm(ks[15], (DEPTH_2, MLA_Q_RANK, MLA_HEADS * MLA_QK_DIM), MLA_Q_RANK ** -0.5),
        'kv_a_norm_g': gain(ks[16], MLA_KV_RANK),
        'w_ukv': nrm(ks[17], (DEPTH_2, MLA_KV_RANK, MLA_HEADS * (MLA_NOPE + MLA_V)), MLA_KV_RANK ** -0.5),
        'q_norm_g': gain(ks[18], MLA_QK_DIM),
        'k_norm_g': gain(ks[19], MLA_QK_DIM),
        'w_out_b': nrm(ks[20], (DEPTH_2, MLA_HEADS * MLA_V, d), (MLA_HEADS * MLA_V) ** -0.5),
        'w_o': nrm(ks[21], (DEPTH_2, d, d), d ** -0.5),
        'router_w': nrm(ks[22], (DEPTH_2, d, N_EXPERTS), d ** -0.5),
        'w_gate': nrm(ks[23], (DEPTH_2, N_EXPERTS, d, EXPERT_FF), d ** -0.5),
        'w_up': nrm(ks[24], (DEPTH_2, N_EXPERTS, d, EXPERT_FF), d ** -0.5),
        'w_down': nrm(ks[25], (DEPTH_2, N_EXPERTS, EXPERT_FF, d), EXPERT_FF ** -0.5),
    }

def second_block(x, c, ctx, c_ctx, ada_w, ada_b, norm1_g, norm2_g, w_in, conv_w, a_log, dt_bias, dn_norm_g,
              w_out_a, q_a_norm_g, w_uq, kv_a_norm_g, w_ukv, q_norm_g, k_norm_g, w_out_b, w_o, router_w,
              w_gate, w_up, w_down):
    b_, n_lat, _ = x.shape
    rows = n_lat // GRID_W
    rope = axial_rope_tables(rows, x.dtype)
    zero_state = jnp.zeros((b_, DN_HEADS, DN_DK, DN_DV), F32)
    for i in range(DEPTH_2):
        last = i == DEPTH_2 - 1
        mod_x = adaln(c, ada_w[i], ada_b[i])
        mod_c = adaln(c_ctx[None], ada_w[i], ada_b[i])

        h_c = modulate(ctx, norm1_g[i], mod_c[0], mod_c[1])
        h_x = modulate(x, norm1_g[i], mod_x[0], mod_x[1])
        qkv_c, z_c, al_c, be_c, cq_c, ckv_c, kr_c, gt_c = jnp.split(h_c @ w_in[i], IN_OFFSETS, axis=-1)
        qkv_x, z_x, al_x, be_x, cq_x, ckv_x, kr_x, gt_x = jnp.split(h_x @ w_in[i], IN_OFFSETS, axis=-1)

        o_dn_c, s_fwd, s_bwd = deltanet_bidir(*deltanet_inputs(qkv_c, al_c, be_c, conv_w[i], a_log[i], dt_bias[i]),
                                              zero_state, zero_state)
        o_dn_x, _, _ = deltanet_bidir(*deltanet_inputs(qkv_x, al_x, be_x, conv_w[i], a_log[i], dt_bias[i]),
                                      s_fwd, s_bwd)

        k_c, v_c = mla_keys_values(ckv_c, kr_c, kv_a_norm_g[i], w_ukv[i], k_norm_g[i], None)
        k_x, v_x = mla_keys_values(ckv_x, kr_x, kv_a_norm_g[i], w_ukv[i], k_norm_g[i], rope)
        q_x = mla_queries(cq_x, q_a_norm_g[i], w_uq[i], q_norm_g[i], rope)
        o_mla_x = softmax_attention(q_x, jnp.concatenate([k_c, k_x], axis=2), jnp.concatenate([v_c, v_x], axis=2))

        mix_x = merge_branches(deltanet_out(o_dn_x, z_x, dn_norm_g[i]), o_mla_x, gt_x, w_out_a[i], w_out_b[i], w_o[i])
        x_mid = x + mod_x[2] * mix_x

        if not last:
            q_c = mla_queries(cq_c, q_a_norm_g[i], w_uq[i], q_norm_g[i], None)
            o_mla_c = softmax_attention(q_c, k_c, v_c)
            mix_c = merge_branches(deltanet_out(o_dn_c, z_c, dn_norm_g[i]), o_mla_c, gt_c,
                                   w_out_a[i], w_out_b[i], w_o[i])
            ctx = ctx + mod_c[2] * mix_c
            ctx = ctx + mod_c[5] * expert_choice_moe(modulate(ctx, norm2_g[i], mod_c[3], mod_c[4]),
                                                     router_w[i], w_gate[i], w_up[i], w_down[i])

        h2 = modulate(x_mid, norm2_g[i], mod_x[3], mod_x[4])
        x = x_mid + mod_x[5] * expert_choice_moe(h2, router_w[i], w_gate[i], w_up[i], w_down[i])
    return x


def setup_inputs(seed=0):
    out = dict(first_inputs(seed))
    for name, value in second_inputs(seed + 1).items():
        if name != "x":
            out[name + "_2"] = value
    return out


def reference(
    x, c, ctx, c_ctx, mod_w, mod_b, norm_pre_mix, norm_post_mix, norm_pre_ffn, norm_post_ffn,
    even_w_in, gla_w_gate, gla_b_gate, gla_out_norm, att_q_norm, att_k_norm, even_w_out,
    odd_w_in, hgrn_lower_bounds, hgrn_out_norm, odd_w_out, ffn_w_gate, ffn_w_up, ffn_w_down,
    c_2, ctx_2, c_ctx_2, ada_w_2, ada_b_2, norm1_g_2, norm2_g_2, w_in_2, conv_w_2, a_log_2,
    dt_bias_2, dn_norm_g_2, w_out_a_2, q_a_norm_g_2, w_uq_2, kv_a_norm_g_2, w_ukv_2, q_norm_g_2,
    k_norm_g_2, w_out_b_2, w_o_2, router_w_2, w_gate_2, w_up_2, w_down_2,
):
    x = first_block(
        x, c, ctx, c_ctx, mod_w, mod_b, norm_pre_mix, norm_post_mix, norm_pre_ffn,
        norm_post_ffn, even_w_in, gla_w_gate, gla_b_gate, gla_out_norm, att_q_norm, att_k_norm,
        even_w_out, odd_w_in, hgrn_lower_bounds, hgrn_out_norm, odd_w_out, ffn_w_gate, ffn_w_up,
        ffn_w_down,
    )
    return second_block(
        x, c_2, ctx_2, c_ctx_2, ada_w_2, ada_b_2, norm1_g_2, norm2_g_2, w_in_2, conv_w_2,
        a_log_2, dt_bias_2, dn_norm_g_2, w_out_a_2, q_a_norm_g_2, w_uq_2, kv_a_norm_g_2,
        w_ukv_2, q_norm_g_2, k_norm_g_2, w_out_b_2, w_o_2, router_w_2, w_gate_2, w_up_2,
        w_down_2,
    )


_drawn_inputs = setup_inputs


def setup_inputs(seed=0):
    import zlib

    import numpy as np

    out = dict(_drawn_inputs(seed))
    spreads = {}
    factors = {'norm_post_mix': 2.925,
     'norm_pre_ffn': 2.74,
     'norm_post_ffn': 3.254,
     'gla_b_gate': 5.496,
     'gla_out_norm': 4.129,
     'att_q_norm': 8.0,
     'att_k_norm': 8.0,
     'hgrn_lower_bounds': 8.0,
     'hgrn_out_norm': 4.314,
     'ctx_2': 3.491,
     'ada_b_2': 3.054,
     'norm1_g_2': 7.563,
     'norm2_g_2': 4.283,
     'dn_norm_g_2': 8.0,
     'q_a_norm_g_2': 8.0,
     'kv_a_norm_g_2': 8.0,
     'q_norm_g_2': 8.0,
     'k_norm_g_2': 8.0}
    for name, (base, spread) in spreads.items():
        noise = np.random.default_rng([zlib.crc32(name.encode()), seed]).standard_normal(out[name].shape)
        drawn = base * np.exp(spread * noise) if base else spread * noise
        out[name] = jnp.asarray(drawn.astype(out[name].dtype))
    for name, factor in factors.items():
        out[name] = (out[name] * factor).astype(out[name].dtype)
    return out
```

```python
import contextlib

import concourse.bass as bass
from concourse import mybir

F32 = mybir.dt.float32
U32 = mybir.dt.uint32
ALU = mybir.AluOpType
ACT = mybir.ActivationFunctionType
AX = mybir.AxisListType

P = 128
D = 1024
KD = D // P
CTX, LAT = 256, 512
N_TOK = CTX + LAT
TILES = N_TOK // P
CTX_TILES = CTX // P
DFF = 2816
EPS = 1e-6


@contextlib.contextmanager
def phase(nc, name, *signals):
    with contextlib.ExitStack() as stack:
        sems, every = {}, []
        for signal in (*signals, "passed"):
            what, _, count = signal.partition("*")
            made = [stack.enter_context(nc.semaphore(f"{name}_{what}{n}")) for n in range(int(count or 1))]
            every += made
            sems[what] = made if count else made[0]
        with nc.Block() as block:
            yield block, sems
        for sem in every:
            nc.sync.sem_clear(sem)
        nc.all_engine_barrier()


class Steps:

    def __init__(self, eng, sem):
        self.eng, self.sem, self.n = eng, sem, 0

    def mark(self, ins):
        self.n += 1
        return ins.then_inc(self.sem, 1)

    def settle(self):
        if self.n:
            self.eng.wait_ge(self.sem, self.n)

    def then(self, ins):
        self.mark(ins)
        self.settle()

    def restart(self):
        self.settle()
        if self.n:
            self.eng.sem_clear(self.sem)
        self.n = 0


def wait_alone(eng, sem, value, passed):
    eng.wait_ge(sem, value)
    eng.sem_inc(passed, 1)


def blocks_of(eng, total, width):
    full, rest = divmod(total, width)
    pairs = full // 2
    if pairs:
        with eng.Fori(0, pairs) as i:
            for s in range(2):
                yield 2 * i + s, s, i, width
    for b in range(2 * pairs, full + (rest > 0)):
        yield b, b % 2, b // 2, width if b < full else rest


def modulation(nc, tag, cond_lat, cond_ctx, w, bias, mod):
    width = 512
    GROUPS = 4
    part = width // GROUPS
    n_out = w.shape[1]
    blocks = n_out // width
    with (
        nc.sbuf_tensor(f"{tag}_c", [P, 2, KD], F32) as c,
        nc.sbuf_tensor(f"{tag}_e", [P, 2, KD], F32) as e,
        nc.sbuf_tensor(f"{tag}_sc", [P, 2, KD], F32) as sc,
        nc.sbuf_tensor(f"{tag}_w", [P, 3, KD, width], F32) as wt,
        nc.sbuf_tensor(f"{tag}_bias", [P, blocks, part], F32) as bt,
        nc.sbuf_tensor(f"{tag}_out", [P, blocks, part], F32) as ot,
        nc.psum_tensor(f"{tag}_ps", [P, 2, GROUPS, 512], F32) as ps,
        phase(nc, tag, "cond_in", "bias_in", "w_in*3", "exp_done", "own", "sc_done", "mm_done", "sum_done", "stored") as (block, S),
    ):
        w_v = w.rearrange("(p k) n -> p k n", k=KD)
        bias_v = bias.rearrange("(a b g c) -> g a b c", a=1, b=blocks, g=GROUPS)
        mod_v = mod.rearrange("r (b g c) -> g r b c", b=blocks, g=GROUPS)
        rows = [slice(P // GROUPS * g, P // GROUPS * g + 2) for g in range(GROUPS)]

        @block.sync
        def _(sp):
            sp.dma_start(c[:, 0, :], cond_lat.rearrange("(p k) -> p k", k=KD)).then_inc(S["cond_in"], 16)
            sp.dma_start(c[:, 1, :], cond_ctx.rearrange("(p k) -> p k", k=KD)).then_inc(S["cond_in"], 16)
            with sp.Fori(0, blocks // 3) as i:
                for s in range(3):
                    sp.wait_ge(S["mm_done"], 3 * i + s + 1)
                    sp.dma_start(wt[:, s, :, :], w_v[:, :, bass.ts(3 * i + s, width)]).then_inc(S["w_in"][s], 16)
            sp.wait_ge(S["sum_done"], blocks + 2)
            for g in range(GROUPS):
                sp.dma_start(mod_v[g], ot[rows[g], :, :]).then_inc(S["stored"], 16)
            sp.wait_ge(S["stored"], 16 * GROUPS)

        @block.scalar
        def _(act):
            for g in range(GROUPS):
                act.dma_start(bt[rows[g], :, :], bias_v[g].broadcast_to([2, blocks, part])).then_inc(S["bias_in"], 16)
            act.wait_ge(S["cond_in"], 32)
            nc.scalar.activation(e[:, :, :], c[:, :, :], ACT.Exp, scale=-1.0).then_inc(S["exp_done"], 1)

        @block.tensor
        def _(pe):
            pe.sem_inc(S["mm_done"], 3)
            pe.wait_ge(S["sc_done"], 1)
            with pe.Fori(0, blocks // 6) as j:
                for u in range(6):
                    s, q = u % 3, u % 2
                    pe.wait_ge(S["w_in"][s], (2 * j + u // 3 + 1) * 16)
                    pe.wait_ge(S["sum_done"], 6 * j + u + 1)
                    for k in range(KD):
                        for g in range(GROUPS):
                            last = nc.tensor.matmul(ps[rows[g], q, g, 0:part], sc[:, :, k], wt[:, s, k, g * part:(g + 1) * part], start=k == 0, stop=k == KD - 1)
                    last.then_inc(S["mm_done"], 1)

        @block.vector
        def _(dve):
            own = Steps(dve, S["own"])
            dve.sem_inc(S["sum_done"], 2)
            dve.wait_ge(S["exp_done"], 1)
            own.then(nc.vector.tensor_scalar(e[:, :, :], e[:, :, :], 1.0, None, ALU.add))
            own.then(nc.vector.reciprocal(e[:, :, :], e[:, :, :]))
            nc.vector.tensor_tensor(sc[:, :, :], c[:, :, :], e[:, :, :], ALU.mult).then_inc(S["sc_done"], 1)
            dve.wait_ge(S["bias_in"], 16 * GROUPS)
            with dve.Fori(0, blocks // 2) as i:
                for q in range(2):
                    dve.wait_ge(S["mm_done"], 2 * i + q + 4)
                    for g in range(GROUPS):
                        last = nc.vector.tensor_tensor(ot[rows[g], bass.ds(2 * i + q, 1), :].rearrange("p b c -> p (b c)"), ps[rows[g], q, g, 0:part],
                                                       bt[rows[g], bass.ds(2 * i + q, 1), :].rearrange("p b c -> p (b c)"), ALU.add)
                    last.then_inc(S["sum_done"], 1)


def linear(nc, tag, xT, kt, w, tiles, tile0=0, out=None, out_sb=None, width=512, rows="(p k) n -> p k n"):
    n = w.shape[1]
    even, odd = (tiles + 1) // 2, tiles // 2
    total = -(-n // width)
    w_v = w.rearrange(rows, p=P)
    k_parts = ((0, kt // 2), (kt // 2, kt))
    with contextlib.ExitStack() as stack:
        wt = stack.enter_context(nc.sbuf_tensor(f"{tag}_w", [P, 2, kt, width], F32))
        stage = out_sb
        if out_sb is None:
            stage = stack.enter_context(nc.sbuf_tensor(f"{tag}_stage", [P, 2, tiles, width], F32))
            out_v = out.rearrange("(m p) n -> p m n", p=P)
        ps = stack.enter_context(nc.psum_tensor(f"{tag}_ps", [P, 8, 512], F32))
        block, S = stack.enter_context(phase(nc, tag, "w_in*4", "w_used", "mm_done", "even_out", "odd_out", "stored*2"))

        @block.sync
        def _(sp):
            for b, s, turn, wd in blocks_of(sp, n, width):
                sp.wait_ge(S["w_used"], b + 1)
                for part, (k0, k1) in enumerate(k_parts):
                    sp.dma_start(wt[:, s, k0:k1, 0:wd], w_v[:, k0:k1, bass.ds(b * width, wd)]).then_inc(S["w_in"][2 * s + part], 16)

        @block.tensor
        def _(pe):
            pe.sem_inc(S["w_used"], 2)
            for b, s, turn, wd in blocks_of(pe, n, width):
                for m in range(tiles):
                    if m % 2 == 0:
                        pe.wait_ge(S["even_out"], b * even + m // 2 + 1)
                    else:
                        pe.wait_ge(S["odd_out"], b * odd + m // 2 + 1)
                    for k in range(kt):
                        for part, (k0, k1) in enumerate(k_parts):
                            if m == 0 and k == k0:
                                pe.wait_ge(S["w_in"][2 * s + part], (turn + 1) * 16)
                        last = nc.tensor.matmul(ps[:, m, 0:wd], xT[:, k, (tile0 + m) * P:(tile0 + m + 1) * P],
                                                wt[:, s, k, 0:wd], start=k == 0, stop=k == kt - 1)
                    if m < tiles - 1:
                        last.then_inc(S["mm_done"], 1)
                last.then_inc(S["mm_done"], 1)
                pe.wait_ge(S["mm_done"], (b + 1) * tiles)
                pe.sem_inc(S["w_used"], 1)

        def copy_out(eng, copy, first, count, done, store=None):
            eng.sem_inc(done, count)
            for b, s, turn, wd in blocks_of(eng, n, width):
                if out_sb is None:
                    eng.wait_ge(S["stored"][s], turn * 16 + 16)
                for m in range(first, tiles, 2):
                    eng.wait_ge(S["mm_done"], b * tiles + m + 1)
                    dst = stage[:, m, bass.ds(b * width, wd)] if out_sb is not None else stage[:, s, m, 0:wd]
                    copy(dst, ps[:, m, 0:wd]).then_inc(done, 1)
                if store:
                    eng.wait_ge(S["even_out"], (b + 2) * even)
                    eng.wait_ge(S["odd_out"], (b + 2) * odd)
                    store(b, s, wd)

        @block.vector
        def _(dve):
            copy_out(dve, nc.vector.tensor_copy, 0, even, S["even_out"])

        @block.scalar
        def _(act):
            if out_sb is not None:
                copy_out(act, nc.scalar.copy, 1, odd, S["odd_out"])
                return
            for s in range(2):
                act.sem_inc(S["stored"][s], 16)

            def store(b, s, wd):
                act.dma_start(out_v[:, tile0:tile0 + tiles, bass.ds(b * width, wd)], stage[:, s, :, 0:wd]).then_inc(S["stored"][s], 16)

            copy_out(act, nc.scalar.copy, 1, odd, S["odd_out"], store)
            for s in range(2):
                act.wait_ge(S["stored"][s], 16 + 16 * ((total + 1 - s) // 2))




def column(vector):
    return vector.rearrange("(p k) -> p k", p=P)


def over_partitions(vector, parts=P):
    return vector.rearrange("(a n) -> a n", a=1).broadcast_to([parts, vector.shape[0]])


def modulated_norm(nc, tag, x, hT, ident, gain, mod, shift_at, scale_at, tile0=0, x_hat=None):
    tiles = TILES - tile0
    with (
        nc.sbuf_tensor(f"{tag}_cols", [P, 5, KD], F32) as cols,
        nc.sbuf_tensor(f"{tag}_mul", [P, 2, KD], F32) as mul,
        nc.sbuf_tensor(f"{tag}_sq", [P, D], F32) as sq,
        nc.sbuf_tensor(f"{tag}_ss", [P, 3, TILES], F32) as ss,
        nc.sbuf_tensor(f"{tag}_xn", [P, 2, D], F32) as xn_slots,
        nc.psum_tensor(f"{tag}_ps", [P, 4, 512], F32) as ps,
        phase(nc, tag, "cols_in", "squares", "mean_done", "root_done", "scaled", "turned", "taken", "own", "own_act") as (block, S),
    ):
        def xn(t):
            return x_hat[:, t, :] if x_hat is not None else xn_slots[:, t % 2, :]

        @block.sync
        def _(sp):
            sp.dma_start(cols[:, 0, :], column(gain)).then_inc(S["cols_in"], 16)
            for row in range(2):
                sp.dma_start(cols[:, 1 + row, :], column(mod[row, scale_at * D:(scale_at + 1) * D])).then_inc(S["cols_in"], 16)
                sp.dma_start(cols[:, 3 + row, :], column(mod[row, shift_at * D:(shift_at + 1) * D])).then_inc(S["cols_in"], 16)

        @block.scalar
        def _(act):
            own = Steps(act, S["own_act"])
            for t in range(tile0, TILES):
                own.settle()
                own.mark(nc.scalar.activation(sq[:, :], x[:, t, :], ACT.Square, accum_out=ss[:, 0, t:t + 1]))
            own.settle()
            act.sem_inc(S["squares"], 1)
            act.wait_ge(S["mean_done"], 1)
            nc.scalar.activation(ss[:, 2, tile0:], ss[:, 1, tile0:], ACT.Sqrt).then_inc(S["root_done"], 1)
            act.wait_ge(S["mean_done"], 2)
            for t in range(tile0, TILES):
                row = 1 if t < CTX_TILES else 0
                for half in range(2):
                    n = 2 * (t - tile0) + half
                    act.wait_ge(S["turned"], n + 1)
                    for k in range(4):
                        kk = 4 * half + k
                        last = nc.scalar.activation(hT[:, kk, t * P:(t + 1) * P], ps[:, n % 4, k * P:(k + 1) * P], ACT.Identity,
                                                    scale=mul[:, row, kk:kk + 1], bias=cols[:, 3 + row, kk:kk + 1])
                        own.mark(last)
                    own.settle()
                    act.sem_inc(S["taken"], 1)

        @block.vector
        def _(dve):
            own = Steps(dve, S["own"])
            dve.wait_ge(S["squares"], 1)
            nc.vector.tensor_scalar(ss[:, 1, tile0:], ss[:, 0, tile0:], 1.0 / D, EPS, ALU.mult, ALU.add).then_inc(S["mean_done"], 1)
            dve.wait_ge(S["cols_in"], 16 * 5)
            for row in range(2):
                own.mark(nc.vector.scalar_tensor_tensor(mul[:, row, :], cols[:, 1 + row, :], 1.0, cols[:, 0, :], ALU.add, ALU.mult))
            own.settle()
            dve.sem_inc(S["mean_done"], 1)
            dve.wait_ge(S["root_done"], 1)
            own.then(nc.vector.reciprocal(ss[:, 1, tile0:], ss[:, 2, tile0:]))
            for t in range(tile0, TILES):
                if x_hat is None and t - tile0 >= 2:
                    dve.wait_ge(S["turned"], 2 * (t - tile0 - 1))
                nc.vector.tensor_scalar(xn(t), x[:, t, :], ss[:, 1, t:t + 1], None, ALU.mult).then_inc(S["scaled"], 1)

        @block.tensor
        def _(pe):
            for t in range(tile0, TILES):
                pe.wait_ge(S["scaled"], t - tile0 + 1)
                for half in range(2):
                    n = 2 * (t - tile0) + half
                    if n >= 4:
                        pe.wait_ge(S["taken"], n - 3)
                    for k in range(4):
                        kk = 4 * half + k
                        last = nc.tensor.transpose(ps[:, n % 4, k * P:(k + 1) * P], xn(t)[:, kk::KD], ident)
                    last.then_inc(S["turned"], 1)


def gated_residual(nc, tag, x, y, mod, gate_at, gain=None, tile0=0):
    normed = gain is not None
    with (
        nc.sbuf_tensor(f"{tag}_gate", [P, 3, D], F32) as gates,
        nc.sbuf_tensor(f"{tag}_tmp", [P, 2, D], F32) as tmp,
        nc.sbuf_tensor(f"{tag}_ss", [P, 3, TILES], F32) as ss,
        phase(nc, tag, "gates_in", "squares", "mean_done", "root_done", "own", "own_act") as (block, S),
    ):
        @block.sync
        def _(sp):
            for row in range(2):
                sp.dma_start(gates[:, row, :], over_partitions(mod[row, gate_at * D:(gate_at + 1) * D])).then_inc(S["gates_in"], 16)
            if normed:
                sp.dma_start(gates[:, 2, :], over_partitions(gain)).then_inc(S["gates_in"], 16)

        if normed:
            @block.scalar
            def _(act):
                own = Steps(act, S["own_act"])
                for t in range(tile0, TILES):
                    own.settle()
                    own.mark(nc.scalar.activation(tmp[:, 0, :], y[:, t - tile0, :], ACT.Square, accum_out=ss[:, 0, t:t + 1]))
                own.settle()
                act.sem_inc(S["squares"], 1)
                act.wait_ge(S["mean_done"], 1)
                nc.scalar.activation(ss[:, 2, tile0:], ss[:, 1, tile0:], ACT.Sqrt).then_inc(S["root_done"], 1)

        @block.vector
        def _(dve):
            own = Steps(dve, S["own"])
            dve.wait_ge(S["gates_in"], 16 * (3 if normed else 2))
            if normed:
                for row in range(2):
                    own.mark(nc.vector.tensor_tensor(gates[:, row, :], gates[:, row, :], gates[:, 2, :], ALU.mult))
                dve.wait_ge(S["squares"], 1)
                nc.vector.tensor_scalar(ss[:, 1, tile0:], ss[:, 0, tile0:], 1.0 / D, EPS, ALU.mult, ALU.add).then_inc(S["mean_done"], 1)
                dve.wait_ge(S["root_done"], 1)
                own.mark(nc.vector.reciprocal(ss[:, 1, tile0:], ss[:, 2, tile0:]))
                own.settle()
            for t in range(tile0, TILES):
                gate = gates[:, 1 if t < CTX_TILES else 0, :]
                if t - tile0 >= 1:
                    own.settle()
                if normed:
                    own.mark(nc.vector.scalar_tensor_tensor(tmp[:, t % 2, :], y[:, t - tile0, :], ss[:, 1, t:t + 1], gate, ALU.mult, ALU.mult))
                else:
                    own.mark(nc.vector.tensor_tensor(tmp[:, t % 2, :], y[:, t - tile0, :], gate, ALU.mult))
                own.settle()
                own.mark(nc.vector.tensor_tensor(x[:, t, :], x[:, t, :], tmp[:, t % 2, :], ALU.add))
            own.settle()


def gate_up(nc, tag, hT, w_gate, w_up, hid, tok0):
    width = 256
    f_tiles = width // P
    n_tok = N_TOK - tok0
    halves = 2 if n_tok > 512 else 1
    span = n_tok // halves
    groups = f_tiles * halves
    wg_v = w_gate.rearrange("(p k) n -> p k n", p=P)
    wu_v = w_up.rearrange("(p k) n -> p k n", p=P)
    ff = w_gate.shape[1]
    hid_flat = hid[:, :, :].rearrange("p f t -> p (f t)")
    with (
        nc.sbuf_tensor(f"{tag}_w", [P, 2, 2, KD, width], F32) as wt,
        nc.sbuf_tensor(f"{tag}_act", [P, 4, span], F32) as silu,
        nc.psum_tensor(f"{tag}_ps", [P, 8, 512], F32) as ps,
        phase(nc, tag, "w_in*4", "w_used", "gate_mm", "up_mm", "silu_done", "product_done") as (block, S),
    ):
        @block.sync
        def _(sp):
            for b, s, turn, wd in blocks_of(sp, ff, width):
                sp.wait_ge(S["w_used"], b + 1)
                for g, v in enumerate((wg_v, wu_v)):
                    sp.dma_start(wt[:, s, g, :, :], v[:, :, bass.ds(b * width, width)]).then_inc(S["w_in"][2 * s + g], 16)

        @block.tensor
        def _(pe):
            pe.sem_inc(S["w_used"], 2)
            for b, s, turn, wd in blocks_of(pe, ff, width):
                for f in range(f_tiles):
                    for h in range(halves):
                        u = f * halves + h
                        cols = slice(tok0 + h * span, tok0 + (h + 1) * span)
                        for g, done in enumerate((S["gate_mm"], S["up_mm"])):
                            pe.wait_ge(S["silu_done"] if g == 0 else S["product_done"], b * groups + u + 1)
                            if u == 0:
                                pe.wait_ge(S["w_in"][2 * s + g], (turn + 1) * 16)
                            for k in range(KD):
                                last = nc.tensor.matmul(ps[:, 2 * (u % 4) + g, 0:span], wt[:, s, g, k, f * P:(f + 1) * P],
                                                        hT[:, k, cols], start=k == 0, stop=k == KD - 1)
                            last.then_inc(done, 1)
                pe.wait_ge(S["up_mm"], (b + 1) * groups)
                pe.sem_inc(S["w_used"], 1)

        @block.scalar
        def _(act):
            act.sem_inc(S["silu_done"], groups)
            for b, s, turn, wd in blocks_of(act, ff, width):
                for u in range(groups):
                    act.wait_ge(S["gate_mm"], b * groups + u + 1)
                    act.wait_ge(S["product_done"], b * groups + u + 1)
                    nc.scalar.activation(silu[:, u, :], ps[:, 2 * u, 0:span], ACT.Silu).then_inc(S["silu_done"], 1)

        @block.vector
        def _(dve):
            dve.sem_inc(S["product_done"], groups)
            for b, s, turn, wd in blocks_of(dve, ff, width):
                for u in range(groups):
                    f, h = divmod(u, halves)
                    dve.wait_ge(S["up_mm"], b * groups + u + 1)
                    dve.wait_ge(S["silu_done"], b * groups + u + 1 + groups)
                    dst = hid_flat[:, bass.ds((b * f_tiles + f) * N_TOK + tok0 + h * span, span)]
                    nc.vector.tensor_tensor(dst, silu[:, u, :], ps[:, 2 * u + 1, 0:span], ALU.mult).then_inc(S["product_done"], 1)


def feed_forward(nc, tag, x, hT, ident, gain_pre, gain_post, mod, w_gate, w_up, w_down, tile0):
    modulated_norm(nc, f"{tag}_norm", x, hT, ident, gain_pre, mod, 3, 4, tile0)
    with nc.sbuf_tensor(f"{tag}_hid", [P, DFF // P, N_TOK], F32) as hid:
        gate_up(nc, f"{tag}_up", hT, w_gate, w_up, hid, tile0 * P)
        y = hT[:, :, :].rearrange("p k t -> p (k t)").rearrange("p (m d) -> p m d", d=D)
        linear(nc, f"{tag}_down", hid, DFF // P, w_down, TILES - tile0, tile0, out_sb=y, width=256, rows="(k p) n -> p k n")
    gated_residual(nc, f"{tag}_res", x, y, mod, 5, gain_post, tile0)




def attention(nc, tag, q, k, v, out_sb, out_at, ident, heads, group, dh, dv, v_stride, v_at, tile0=0):
    scale = dh ** -0.5
    dims = [(d, min(P, dh - d)) for d in range(0, dh, P)]
    nd = len(dims)
    q_tiles = list(range(tile0, TILES))
    nq = len(q_tiles)
    span = N_TOK // 2

    k_jobs = [(d, m, min(m + 4, TILES)) for d in range(nd) for m in range(0, TILES, 4)]
    q_jobs = [(d, m, min(m + 4, TILES)) for d in range(nd) for m in range(tile0, TILES, 4)]
    if (len(k_jobs) + len(q_jobs)) % 2:
        d, m, end = q_jobs.pop()
        q_jobs += [(d, m, m + 1), (d, m + 1, end)]
    n_kq = len(k_jobs) + len(q_jobs)
    key_tiles = {t: CTX_TILES if t < CTX_TILES else TILES for t in q_tiles}
    p_jobs = {t: [(m, min(m + 4, key_tiles[t])) for m in range(0, key_tiles[t], 4)] for t in q_tiles}
    p_first, nj = {}, n_kq
    for t in q_tiles:
        p_first[t] = nj
        nj += len(p_jobs[t])
    assert nj % 2 == 0 and nq % 2 == 0
    n_st = 3 if nq % 3 == 0 else 4
    assert nq % n_st == 0

    def heads_of(eng):
        if group == 1:
            with eng.Fori(0, heads // 2) as i:
                for s in range(2):
                    yield 2 * i + s, i, s, 2 * i + s
        else:
            with eng.Fori(0, heads // group) as kv:
                with eng.Fori(0, group // 2) as j:
                    for s in range(2):
                        yield kv * group + 2 * j + s, kv * (group // 2) + j, s, kv

    with (
        nc.sbuf_tensor(f"{tag}_q", [P, 2, TILES, dh], F32) as q_tok,
        nc.sbuf_tensor(f"{tag}_k", [P, 2, TILES, dh], F32) as k_tok,
        nc.sbuf_tensor(f"{tag}_v", [P, 2, TILES, dv], F32) as v_tok,
        nc.sbuf_tensor(f"{tag}_qT", [P, nd, N_TOK], F32) as qT,
        nc.sbuf_tensor(f"{tag}_kT", [P, nd, N_TOK], F32) as kT,
        nc.sbuf_tensor(f"{tag}_p", [P, 2, N_TOK], F32) as probs,
        nc.sbuf_tensor(f"{tag}_pT", [P, 2, N_TOK], F32) as probsT,
        nc.sbuf_tensor(f"{tag}_st", [P, n_st, 4], F32) as st,
        nc.psum_tensor(f"{tag}_ps", [P, 8, 512], F32) as ps,
        phase(nc, tag, "head_in*2", "turned", "taken", "scores", "max_done", "exp_done", "pv_done", "normed", "own") as (block, S),
    ):
        q_v = q.rearrange("(m p) c -> p m c", p=P)
        k_v = k.rearrange("(m p) c -> p m c", p=P)
        v_v = v.rearrange("(m p) c -> p m c", p=P)

        @block.sync
        def _(sp):
            for h, turn, s, kv in heads_of(sp):
                sp.wait_ge(S["pv_done"], h * nq + nq)
                sp.dma_start(k_tok[:, s, :, :], k_v[:, :, bass.ds(kv * dh, dh)]).then_inc(S["head_in"][s], 16)
                sp.dma_start(q_tok[:, s, tile0:, :], q_v[:, tile0:, bass.ds(h * dh, dh)]).then_inc(S["head_in"][s], 16)
                sp.dma_start(v_tok[:, s, :, :], v_v[:, :, bass.ds(v_at + kv * v_stride, dv)]).then_inc(S["head_in"][s], 16)

        @block.tensor
        def _(pe):
            pe.sem_inc(S["turned"], nj)
            pe.sem_inc(S["pv_done"], 2 * nq)
            for h, turn, s, kv in heads_of(pe):
                pe.wait_ge(S["head_in"][s], (turn + 1) * 48)
                for j, (d, m0, m1) in enumerate(k_jobs + q_jobs):
                    src = k_tok if j < len(k_jobs) else q_tok
                    at, w = dims[d]
                    wait_alone(pe, S["taken"], h * nj + j + 1, S["passed"])
                    for m in range(m0, m1):
                        last = nc.tensor.transpose(ps[0:w, j % 2, (m - m0) * P:(m - m0 + 1) * P], src[:, s, m, at:at + w], ident)
                    last.then_inc(S["turned"], 1)
                pe.wait_ge(S["taken"], h * nj + n_kq + 2)
                for n in range(nq + 2):
                    if n < nq:
                        t = q_tiles[n]
                        pe.wait_ge(S["exp_done"], h * nq + n + 1)
                        for half in range(2 if key_tiles[t] == TILES else 1):
                            wd = span if key_tiles[t] == TILES else CTX
                            for d, (at, w) in enumerate(dims):
                                last = nc.tensor.matmul(ps[:, 2 + 2 * (n % 2) + half, 0:wd], qT[0:w, d, t * P:(t + 1) * P],
                                                        kT[0:w, d, half * span:half * span + wd], start=d == 0, stop=d == nd - 1)
                        last.then_inc(S["scores"], 1)
                    if 1 <= n <= nq:
                        t = q_tiles[n - 1]
                        pe.wait_ge(S["exp_done"], h * nq + n + 2)
                        for j, (m0, m1) in enumerate(p_jobs[t]):
                            j += p_first[t]
                            pe.wait_ge(S["taken"], h * nj + j + 1)
                            for m in range(m0, m1):
                                last = nc.tensor.transpose(ps[:, j % 2, (m - m0) * P:(m - m0 + 1) * P],
                                                           probs[:, (n - 1) % 2, m * P:(m + 1) * P], ident)
                            last.then_inc(S["turned"], 1)
                    if n >= 2:
                        t = q_tiles[n - 2]
                        pe.wait_ge(S["taken"], h * nj + p_first[t] + len(p_jobs[t]) + 2)
                        pe.wait_ge(S["normed"], h * nq + n - 3 + n_st)
                        for m in range(key_tiles[t]):
                            last = nc.tensor.matmul(ps[:, 6 + n % 2, 0:dv], probsT[:, n % 2, m * P:(m + 1) * P],
                                                    v_tok[:, s, m, :], start=m == 0, stop=m == key_tiles[t] - 1)
                        last.then_inc(S["pv_done"], 1)

        def score_banks(n):
            b = 2 + 2 * (n % 2)
            if key_tiles[q_tiles[n]] == TILES:
                return ps[:, b:b + 2, 0:span]
            return ps[:, b, 0:CTX]

        def probs_of(n):
            if key_tiles[q_tiles[n]] == TILES:
                return probs[:, n % 2, :].rearrange("p (b k) -> p b k", b=2)
            return probs[:, n % 2, 0:CTX]

        @block.scalar
        def _(act):
            act.sem_inc(S["exp_done"], 2)
            for h, turn, s, kv in heads_of(act):
                for n in range(nq):
                    act.wait_ge(S["max_done"], h * nq + n + 1)
                    if n >= 2:
                        before = q_tiles[n - 2]
                        act.wait_ge(S["turned"], h * nj + nj + p_first[before] + len(p_jobs[before]))
                    else:
                        before = q_tiles[nq - 2 + n]
                        act.wait_ge(S["turned"], h * nj + p_first[before] + len(p_jobs[before]))
                    act.wait_ge(S["normed"], h * nq + n + 1)
                    nc.scalar.activation(probs_of(n), score_banks(n), ACT.Exp, bias=st[:, n % n_st, 1:2], scale=scale,
                                         accum_out=st[:, n % n_st, 2:3]).then_inc(S["exp_done"], 1)

        @block.vector
        def _(dve):
            own = Steps(dve, S["own"])
            dve.sem_inc(S["taken"], 2)
            dve.sem_inc(S["normed"], n_st)
            for h, turn, s, kv in heads_of(dve):
                for j, (d, m0, m1) in enumerate(k_jobs + q_jobs):
                    dst = kT if j < len(k_jobs) else qT
                    at, w = dims[d]
                    dve.wait_ge(S["turned"], h * nj + nj + j + 1)
                    nc.vector.tensor_copy(dst[0:w, d, m0 * P:m1 * P], ps[0:w, j % 2, 0:(m1 - m0) * P]).then_inc(S["taken"], 1)
                for n in range(nq + 2):
                    if n < nq:
                        dve.wait_ge(S["scores"], h * nq + n + 1)
                        dve.wait_ge(S["exp_done"], h * nq + n + 1)
                        own.then(nc.vector.tensor_reduce(st[:, n % n_st, 0:1], score_banks(n), AX.XY if key_tiles[q_tiles[n]] == TILES else AX.X, ALU.max))
                        nc.vector.tensor_scalar(st[:, n % n_st, 1:2], st[:, n % n_st, 0:1], -scale, None, ALU.mult).then_inc(S["max_done"], 1)
                    if 1 <= n <= nq:
                        t = q_tiles[n - 1]
                        dve.wait_ge(S["pv_done"], h * nq + 2 * nq + n - 2)
                        for j, (m0, m1) in enumerate(p_jobs[t]):
                            j += p_first[t]
                            dve.wait_ge(S["turned"], h * nj + nj + j + 1)
                            nc.vector.tensor_copy(probsT[:, (n - 1) % 2, m0 * P:m1 * P], ps[:, j % 2, 0:(m1 - m0) * P]).then_inc(S["taken"], 1)
                    if n >= 2:
                        t, r = q_tiles[n - 2], st[:, (n - 2) % n_st, :]
                        dve.wait_ge(S["pv_done"], h * nq + 2 * nq + n - 1)
                        own.then(nc.vector.reciprocal(r[:, 3:4], r[:, 2:3]))
                        nc.vector.tensor_scalar(out_sb[:, t, bass.ds(out_at + h * dv, dv)], ps[:, 6 + n % 2, 0:dv], r[:, 3:4], None, ALU.mult).then_inc(S["normed"], 1)
                own.restart()



LEVELS = 7

IDENT = 0
UPTO = (1, 2)
AFTER = (3, 4)
BETWEEN = (5, 5 + LEVELS)
PAIR = (5 + 2 * LEVELS, 5 + 3 * LEVELS)
N_TABLES = 5 + 4 * LEVELS


def tables():
    import numpy as np

    a, b = np.meshgrid(np.arange(P), np.arange(P), indexing="ij")
    t = np.zeros((N_TABLES, P, P), np.float32)
    t[IDENT] = a == b
    t[UPTO[0]], t[UPTO[1]] = a <= b, a >= b
    t[AFTER[0]], t[AFTER[1]] = a > b, a < b
    for level in range(LEVELS):
        half = 1 << level
        same = a // (2 * half) == b // (2 * half)
        middle = b // (2 * half) * 2 * half + half
        right_a, right_b = a // half % 2 == 1, b // half % 2 == 1
        t[BETWEEN[0] + level] = np.where(right_b, (a >= middle) & (a <= b), (a > b) & (a < middle))
        t[BETWEEN[1] + level] = np.where(right_b, (a >= middle) & (a < b), (a >= b) & (a < middle))
        t[PAIR[0] + level] = same & ~right_a & right_b
        t[PAIR[1] + level] = same & right_a & ~right_b
    return np.ascontiguousarray(t.transpose(1, 0, 2))


def chunks_of(eng, direction, groups, at_group=None):
    half = TILES // 2

    def group(g):
        if at_group:
            at_group()
        if direction == 0:
            with eng.Fori(0, half) as i:
                for s in range(2):
                    yield g, 2 * i + s, g * TILES + 2 * i + s, g * half + i, s
        else:
            for s in range(CTX_TILES):
                yield g, CTX_TILES - 1 - s, g * TILES + s, g * half, s
            with eng.Fori(1, half) as i:
                for s in range(2):
                    yield g, TILES + CTX_TILES - 1 - s - 2 * i, g * TILES + 2 * i + s, g * half + i, s

    if groups == 1:
        yield from group(0)
    else:
        with eng.Fori(0, groups) as g:
            yield from group(g)


def gated_scan(nc, tag, direction, groups, q, k, g, v, v_at, o_sb, cst):
    d = direction
    H = 4
    W = H * P
    last = P - 1 if d == 0 else 0
    with (
        nc.sbuf_tensor(f"{tag}_q", [P, 2, W], F32) as q_in,
        nc.sbuf_tensor(f"{tag}_k", [P, 2, W], F32) as k_in,
        nc.sbuf_tensor(f"{tag}_g", [P, 2, W], F32) as g_in,
        nc.sbuf_tensor(f"{tag}_v", [P, 2, W], F32) as v_in,
        nc.sbuf_tensor(f"{tag}_qT", [P, W], F32) as qT,
        nc.sbuf_tensor(f"{tag}_kT", [P, W], F32) as kT,
        nc.sbuf_tensor(f"{tag}_eg", [P, 2, W], F32) as eg,
        nc.sbuf_tensor(f"{tag}_er", [P, W], F32) as er,
        nc.sbuf_tensor(f"{tag}_el", [P, 2, W], F32) as el,
        nc.sbuf_tensor(f"{tag}_ql", [P, 2, W], F32) as ql,
        nc.sbuf_tensor(f"{tag}_kl", [P, 2, W], F32) as kl,
        nc.sbuf_tensor(f"{tag}_qg", [P, W], F32) as qg,
        nc.sbuf_tensor(f"{tag}_kd", [P, W], F32) as kd,
        nc.sbuf_tensor(f"{tag}_acc", [P, W], F32) as acc,
        nc.sbuf_tensor(f"{tag}_s", [P, W], F32) as state,
        nc.psum_tensor(f"{tag}_ps", [P, 8, 512], F32) as ps,
        phase(nc, tag, "chunk_in*2", "upto_mm", "after_mm", "turned", "level_mm", "score_mm", "out_mm", "state_mm",
              "eg_done", "er_done", "copied", "level_exp", "kd_done", "qg_done", "scaled", "placed", "out_done",
              "state_done", "eg_used", "own") as (block, S),
    ):
        def head(x, h):
            return x[:, h * P:(h + 1) * P]

        def halves(x, level, second):
            h = 1 << level
            return x.rearrange("p (n s) -> p n s", s=2 * h)[:, :, h * second:h * second + h]

        @block.sync
        def _(sp):
            for gr, c, t, turn, s in chunks_of(sp, d, groups):
                wait_alone(sp, S["state_mm"], t + 1, S["passed"])
                rows, cols = bass.ts(c, P), bass.ds(gr * W, W)
                for dst, src, at in ((g_in, g, cols), (q_in, q, cols), (k_in, k, cols), (v_in, v, bass.ds(v_at + gr * W, W))):
                    sp.dma_start(dst[:, s, :], src[rows, at]).then_inc(S["chunk_in"][s], 16)

        @block.tensor
        def _(pe):
            pe.sem_inc(S["state_mm"], 2)
            for gr, c, t, turn, s in chunks_of(pe, d, groups):
                pe.wait_ge(S["chunk_in"][s], (turn + 1) * 64)
                pe.wait_ge(S["eg_done"], t + 1)
                for h in range(H):
                    mm = nc.tensor.matmul(ps[:, 0, h * P:(h + 1) * P], head(g_in[:, s, :], h), cst[:, UPTO[d], :], start=True, stop=True)
                mm.then_inc(S["upto_mm"], 1)
                pe.wait_ge(S["copied"], 2 * t + 1)
                for b, src in ((2, q_in), (3, k_in)):
                    for h in range(H):
                        mm = nc.tensor.transpose(ps[:, b, h * P:(h + 1) * P], head(src[:, s, :], h), cst[:, IDENT, :])
                    mm.then_inc(S["turned"], 1)
                pe.wait_ge(S["er_done"], t + 1)
                nc.tensor.matmul(ps[:, 1, :], cst[:, AFTER[d], :], g_in[:, s, :], start=True, stop=True).then_inc(S["after_mm"], 1)

                def scores(x, lhs, rhs):
                    if x == 0:
                        pe.wait_ge(S["copied"], 2 * t + 3)
                        pe.wait_ge(S["out_done"], t + 1)
                    else:
                        pe.wait_ge(S["scaled"], LEVELS * t + x + 1)
                        if x == 1:
                            pe.wait_ge(S["state_done"], t + gr + 1)
                        else:
                            pe.wait_ge(S["placed"], (LEVELS + 1) * t + x - 1)
                    for h in range(H):
                        mm = nc.tensor.matmul(ps[:, 6 + x % 2, h * P:(h + 1) * P], head(lhs, h), head(rhs, h), start=True, stop=True)
                    mm.then_inc(S["score_mm"], 1)

                for level in range(LEVELS):
                    pe.wait_ge(S["level_exp"], LEVELS * t + max(level - 1, 0) + 1)
                    for h in range(H):
                        mm = nc.tensor.matmul(ps[:, 4 + level % 2, h * P:(h + 1) * P], head(g_in[:, s, :], h),
                                              cst[:, BETWEEN[d] + level, :], start=True, stop=True)
                    mm.then_inc(S["level_mm"], 1)
                    if level == 0:
                        scores(0, kT[:, :], qT[:, :])
                    else:
                        scores(level, kl[:, (level - 1) % 2, :], ql[:, (level - 1) % 2, :])
                scores(LEVELS, kl[:, (LEVELS - 1) % 2, :], ql[:, (LEVELS - 1) % 2, :])
                pe.wait_ge(S["placed"], (LEVELS + 1) * (t + 1))
                pe.wait_ge(S["qg_done"], t + 1)
                pe.wait_ge(S["state_done"], t + gr + 1)
                for h in range(H):
                    nc.tensor.matmul(ps[:, 6, h * P:(h + 1) * P], head(acc, h), head(v_in[:, s, :], h), start=True, stop=False)
                    mm = nc.tensor.matmul(ps[:, 6, h * P:(h + 1) * P], head(qg, h), head(state, h), start=False, stop=True)
                mm.then_inc(S["out_mm"], 1)
                pe.wait_ge(S["kd_done"], t + 2)
                for h in range(H):
                    mm = nc.tensor.matmul(ps[:, 7, h * P:(h + 1) * P], head(kd, h), head(v_in[:, s, :], h), start=True, stop=True)
                mm.then_inc(S["state_mm"], 1)

        @block.scalar
        def _(act):
            act.sem_inc(S["eg_done"], 1)
            act.sem_inc(S["er_done"], 1)
            act.sem_inc(S["copied"], 1)
            act.sem_inc(S["level_exp"], 1)
            for gr, c, t, turn, s in chunks_of(act, d, groups):
                act.wait_ge(S["upto_mm"], t + 1)
                act.wait_ge(S["eg_used"], t + 1)
                nc.scalar.activation(eg[:, s, :], ps[:, 0, :], ACT.Exp).then_inc(S["eg_done"], 1)
                act.wait_ge(S["scaled"], LEVELS * t + 1)
                for n, (b, dst) in enumerate(((2, qT), (3, kT))):
                    act.wait_ge(S["turned"], 2 * t + n + 1)
                    nc.scalar.copy(dst[:, :], ps[:, b, :]).then_inc(S["copied"], 1)
                act.wait_ge(S["after_mm"], t + 1)
                act.wait_ge(S["kd_done"], t + 1)
                nc.scalar.activation(er[:, :], ps[:, 1, :], ACT.Exp).then_inc(S["er_done"], 1)
                for level in range(LEVELS):
                    act.wait_ge(S["level_mm"], LEVELS * t + level + 1)
                    act.wait_ge(S["scaled"], LEVELS * t + max(level - 1, 0) + 1)
                    nc.scalar.activation(el[:, level % 2, :], ps[:, 4 + level % 2, :], ACT.Exp).then_inc(S["level_exp"], 1)

        @block.vector
        def _(dve):
            own = Steps(dve, S["own"])
            for x in (acc, ql, kl):
                own.mark(nc.vector.memset(x[:], 0.0))
            own.restart()
            dve.sem_inc(S["eg_used"], 2)
            for sem in (S["scaled"], S["kd_done"], S["out_done"], S["score_mm"]):
                dve.sem_inc(sem, 1)

            def new_state():
                own.mark(nc.vector.memset(state[:, :], 0.0))
                own.restart()
                dve.sem_inc(S["state_done"], 1)

            masks = [cst[:, PAIR[d] + level, :] for level in range(LEVELS)]

            def place(t, x):
                if x:
                    dve.wait_ge(S["placed"], (LEVELS + 1) * t + x)
                wait_alone(dve, S["score_mm"], (LEVELS + 1) * t + x + 2, S["passed"])
                mask = cst[:, IDENT, :] if x == 0 else masks[x - 1]
                nc.vector.copy_predicated(acc[:, :].rearrange("p (h i) -> p h i", h=H),
                                          mask.bitcast(U32).unsqueeze(1).broadcast_to([P, H, P]),
                                          ps[:, 6 + x % 2, :].rearrange("p (h i) -> p h i", h=H)).then_inc(S["placed"], 1)

            for gr, c, t, turn, s in chunks_of(dve, d, groups, new_state):
                dve.wait_ge(S["er_done"], t + 2)
                dve.wait_ge(S["chunk_in"][s], (turn + 1) * 64)
                nc.vector.tensor_tensor(kd[:, :], k_in[:, s, :], er[:, :], ALU.mult).then_inc(S["kd_done"], 1)
                dve.wait_ge(S["eg_done"], t + 2)
                dve.wait_ge(S["copied"], 2 * t + 3)
                nc.vector.tensor_tensor(qg[:, :], qT[:, :], eg[:, s, :], ALU.mult).then_inc(S["qg_done"], 1)
                for level in range(LEVELS):
                    dve.wait_ge(S["level_exp"], LEVELS * t + level + 2)
                    dve.wait_ge(S["score_mm"], (LEVELS + 1) * t + level + 1)
                    e = el[:, level % 2, :]
                    own.mark(nc.vector.tensor_tensor(halves(ql[:, level % 2, :], level, 1 - d), halves(qT[:, :], level, 1 - d),
                                                     halves(e, level, 1 - d), ALU.mult))
                    own.mark(nc.vector.tensor_tensor(halves(kl[:, level % 2, :], level, d), halves(kT[:, :], level, d),
                                                     halves(e, level, d), ALU.mult))
                    own.settle()
                    dve.sem_inc(S["scaled"], 1)
                    place(t, level)
                place(t, LEVELS)
                wait_alone(dve, S["out_mm"], t + 1, S["passed"])
                o = o_sb[:, bass.ds(c, 1), bass.ds(gr * W, W)].rearrange("p a w -> p (a w)")
                if d == 0:
                    nc.vector.tensor_copy(o, ps[:, 6, :]).then_inc(S["out_done"], 1)
                else:
                    nc.vector.tensor_tensor(o, ps[:, 6, :], o, ALU.add).then_inc(S["out_done"], 1)
                dve.wait_ge(S["state_mm"], t + 3)
                for h in range(H):
                    own.mark(nc.vector.scalar_tensor_tensor(head(state, h), head(state, h), eg[:, s, h * P + last:h * P + last + 1],
                                                            ps[:, 7, h * P:(h + 1) * P], ALU.mult, ALU.add))
                own.restart()
                dve.sem_inc(S["state_done"], 1)
                dve.sem_inc(S["eg_used"], 1)




def both_ways(eng, groups, at_group):
    half = TILES // 2
    with eng.Fori(0, groups) as g:
        at_group()
        for s in range(CTX_TILES):
            yield g, (s, CTX_TILES - 1 - s), g * TILES + s, g * half, s
        with eng.Fori(1, half) as i:
            for s in range(2):
                yield g, (2 * i + s, TILES + CTX_TILES - 1 - s - 2 * i), g * TILES + 2 * i + s, g * half + i, s


def delta_scan(nc, tag, groups, q, k, v, decay, beta, o_sb, cst):
    H = 4
    W = H * P
    heads = groups * H
    with contextlib.ExitStack() as stack:
        def sb(name, *shape):
            return stack.enter_context(nc.sbuf_tensor(f"{tag}_{name}", [P, *shape], F32))

        q_in = sb("q_in", 2, 2, W)
        k_in = sb("k_in", 2, 2, W)
        v_in = sb("v_in", 2, 2, W)
        ab_in = sb("ab_in", 2, 2, 2 * H)
        grow = sb("grow", 2, W)
        eg = sb("eg", 2, W)
        sm = sb("sm", 2, 2 * H)
        esm = sb("esm", 2, 2 * H)
        fac = sb("fac", 2, 2 * H)
        qT = sb("qT", 2, W)
        kT = sb("kT", 2, W)
        dn = sb("dn", 2, W)
        dt = sb("dt", 2, W)
        neg_m = sb("neg_m", 2, W)
        qk = sb("qk", 2, W)
        T = sb("T", 2, W)
        X = sb("X", 2, W)
        y_sb = sb("y_sb", 2, W)
        kb = sb("kb", 2, W)
        kd = sb("kd", 2, W)
        vb = sb("vb", 2, W)
        nw = sb("nw", 2, W)
        vn = sb("vn", 2, W)
        qe = sb("qe", 2, W)
        state = sb("state", 2, W)
        ps = stack.enter_context(nc.psum_tensor(f"{tag}_ps", [P, 8, 512], F32))
        block, S = stack.enter_context(phase(nc, tag, "in_fwd*2", "in_bwd*2", "row_mm*2", "sums_mm*2", "turned*2", "kk_mm*2", "qk_mm*2", "turned_n*2",
              "y_mm*2", "t_mm*2", "x_mm*2", "w_mm*2", "v_mm*2", "out_mm*2", "state_mm*2",
              "row_copied*2", "eg_done*2", "copied*2", "sums_exp*2", "below_exp*2", "above_exp*2", "y_copied*2", "w_copied*2",
              "sums_copied*2", "below*2", "above*2", "n_done*2", "qk_done*2", "t_placed*2", "x_placed*2", "scaled*2",
              "qe_done*2", "vn_done*2", "out_done*2", "state_done*2", "own"))
        chunk_in = (S["in_fwd"], S["in_bwd"])
        L = LEVELS - 1

        def bank(d, n):
            return 4 * d + n

        def head(x, h):
            return x[:, h * P:(h + 1) * P]

        def by_head(x):
            return x.rearrange("p (h n) -> p h n", h=H)

        def per_head(x):
            return x.unsqueeze(2).broadcast_to([P, H, P])

        @block.sync
        def _(sp):
            for gr, cs, t, turn, s in both_ways(sp, groups, lambda: None):
                for d in range(2):
                    wait_alone(sp, S["state_mm"][d], t + 1, S["passed"])
                    rows, cols = bass.ts(cs[d], P), bass.ds(gr * W, W)
                    for dst, src in ((q_in, q), (k_in, k), (v_in, v)):
                        sp.dma_start(dst[:, d, s, :], src[rows, cols]).then_inc(chunk_in[d][s], 16)
                    for n, src in enumerate((decay, beta)):
                        sp.dma_start(ab_in[:, d, s, n * H:(n + 1) * H], src[rows, bass.ds(d * heads + gr * H, H)]).then_inc(chunk_in[d][s], 16)

        @block.tensor
        def _(pe):
            for d in range(2):
                pe.sem_inc(S["state_mm"][d], 2)
            for gr, cs, t, turn, s in both_ways(pe, groups, lambda: None):
                def mm4(d, b, lhs, rhs, **flags):
                    for h in range(H):
                        mm = nc.tensor.matmul(ps[:, bank(d, b), h * P:(h + 1) * P], head(lhs, h), head(rhs, h), start=True, stop=True)
                    return mm

                for d in range(2):
                    pe.wait_ge(chunk_in[d][s], (turn + 1) * 80)
                    pe.wait_ge(S["vn_done"][d], t + 1)
                    for h in range(H):
                        mm = nc.tensor.matmul(ps[:, bank(d, 0), h * P:(h + 1) * P], ab_in[:, d, s, h:h + 1].broadcast_to([P, P]),
                                              cst[:, UPTO[d], :], start=True, stop=True)
                    mm.then_inc(S["row_mm"][d], 1)
                    pe.wait_ge(S["state_done"][d], t + gr + 1)
                    nc.tensor.matmul(ps[:, bank(d, 1), 0:H], cst[:, UPTO[d], :], ab_in[:, d, s, 0:H], start=True, stop=True)
                    nc.tensor.matmul(ps[:, bank(d, 1), H:2 * H], cst[:, AFTER[d], :], ab_in[:, d, s, 0:H], start=True, stop=True).then_inc(S["sums_mm"][d], 1)
                    for b, src, free in ((2, q_in, S["out_done"]), (3, k_in, S["w_copied"])):
                        pe.wait_ge(free[d], t + 1)
                        for h in range(H):
                            mm = nc.tensor.transpose(ps[:, bank(d, b), h * P:(h + 1) * P], head(src[:, d, s, :], h), cst[:, IDENT, :])
                        mm.then_inc(S["turned"][d], 1)
                for d in range(2):
                    pe.wait_ge(S["copied"][d], 2 * t + 2)
                    pe.wait_ge(S["row_copied"][d], t + 1)
                    mm4(d, 0, kT[:, d, :], kT[:, d, :]).then_inc(S["kk_mm"][d], 1)
                    pe.wait_ge(S["sums_copied"][d], t + 1)
                    mm4(d, 1, kT[:, d, :], qT[:, d, :]).then_inc(S["qk_mm"][d], 1)
                for d in range(2):
                    pe.wait_ge(S["n_done"][d], t + 1)
                    pe.wait_ge(S["qk_done"][d], t + 1)
                    for h in range(H):
                        mm = nc.tensor.transpose(ps[:, bank(d, 1), h * P:(h + 1) * P], head(neg_m[:, d, :], h), cst[:, IDENT, :])
                    mm.then_inc(S["turned_n"][d], 1)
                for level in range(1, LEVELS):
                    for d in range(2):
                        pe.wait_ge(S["x_placed"][d], LEVELS * t + level)
                        if level > 1:
                            pe.wait_ge(S["y_copied"][d], L * t + level - 1)
                        mm4(d, 2, neg_m[:, d, :], X[:, d, :]).then_inc(S["y_mm"][d], 1)
                    for d in range(2):
                        pe.wait_ge(S["y_copied"][d], L * t + level)
                        pe.wait_ge(S["t_placed"][d], L * t + level)
                        mm4(d, 1, T[:, d, :], y_sb[:, d, :]).then_inc(S["x_mm"][d], 1)
                        if level < L:
                            mm4(d, 0, y_sb[:, d, :], T[:, d, :]).then_inc(S["t_mm"][d], 1)
                for d in range(2):
                    pe.wait_ge(S["x_placed"][d], LEVELS * (t + 1))
                    pe.wait_ge(S["scaled"][d], t + 1)
                    mm4(d, 3, kb[:, d, :], X[:, d, :]).then_inc(S["w_mm"][d], 1)
                for d in range(2):
                    pe.wait_ge(S["w_copied"][d], t + 2)
                    pe.wait_ge(S["state_done"][d], t + gr + 1)
                    for h in range(H):
                        out = ps[:, bank(d, 0), h * P:(h + 1) * P]
                        nc.tensor.matmul(out, head(X[:, d, :], h), head(vb[:, d, :], h), start=True, stop=False)
                        mm = nc.tensor.matmul(out, head(nw[:, d, :], h), head(state[:, d, :], h), start=False, stop=True)
                    mm.then_inc(S["v_mm"][d], 1)
                for d in range(2):
                    pe.wait_ge(S["vn_done"][d], t + 2)
                    pe.wait_ge(S["qe_done"][d], t + 1)
                    pe.wait_ge(S["y_copied"][d], L * (t + 1))
                    for h in range(H):
                        out = ps[:, bank(d, 2), h * P:(h + 1) * P]
                        nc.tensor.matmul(out, head(qe[:, d, :], h), head(state[:, d, :], h), start=True, stop=False)
                        mm = nc.tensor.matmul(out, head(qk[:, d, :], h), head(vn[:, d, :], h), start=False, stop=True)
                    mm.then_inc(S["out_mm"][d], 1)
                    mm4(d, 1, kd[:, d, :], vn[:, d, :]).then_inc(S["state_mm"][d], 1)

        @block.scalar
        def _(act):
            for d in range(2):
                act.sem_inc(S["w_copied"][d], 1)
            for gr, cs, t, turn, s in both_ways(act, groups, lambda: None):
                for d in range(2):
                    act.wait_ge(S["row_mm"][d], t + 1)
                    nc.scalar.copy(grow[:, d, :], ps[:, bank(d, 0), :]).then_inc(S["row_copied"][d], 1)
                    act.wait_ge(S["state_done"][d], t + gr + 1)
                    act.wait_ge(S["row_copied"][d], t + 1)
                    nc.scalar.activation(eg[:, d, :], grow[:, d, :], ACT.Exp).then_inc(S["eg_done"][d], 1)
                    for n, dst in enumerate((qT, kT)):
                        act.wait_ge(S["turned"][d], 2 * t + n + 1)
                        nc.scalar.copy(dst[:, d, :], ps[:, bank(d, 2 + n), :]).then_inc(S["copied"][d], 1)
                for d in range(2):
                    act.wait_ge(S["sums_copied"][d], t + 1)
                    nc.scalar.activation(esm[:, d, :], sm[:, d, :], ACT.Exp).then_inc(S["sums_exp"][d], 1)
                    act.wait_ge(S["below"][d], t + 1)
                    nc.scalar.activation(dn[:, d, :], dn[:, d, :], ACT.Exp, scale=-1.0).then_inc(S["below_exp"][d], 1)
                    act.wait_ge(S["above"][d], t + 1)
                    nc.scalar.activation(dt[:, d, :], dt[:, d, :], ACT.Exp).then_inc(S["above_exp"][d], 1)
                for level in range(1, LEVELS):
                    for d in range(2):
                        act.wait_ge(S["y_mm"][d], L * t + level)
                        nc.scalar.copy(y_sb[:, d, :], ps[:, bank(d, 2), :]).then_inc(S["y_copied"][d], 1)
                for d in range(2):
                    act.wait_ge(S["w_mm"][d], t + 1)
                    nc.scalar.mul(nw[:, d, :], ps[:, bank(d, 3), :], -1.0).then_inc(S["w_copied"][d], 1)

        @block.vector
        def _(dve):
            own = Steps(dve, S["own"])
            own.mark(nc.vector.memset(o_sb[:, :, 0:groups * W], 0.0))
            own.restart()
            for d in range(2):
                dve.sem_inc(S["vn_done"][d], 1)
                dve.sem_inc(S["out_done"][d], 1)

            def new_state():
                for d in range(2):
                    own.mark(nc.vector.memset(state[:, d, :], 0.0))
                own.restart()
                for d in range(2):
                    dve.sem_inc(S["state_done"][d], 1)

            def mask(n):
                return cst[:, n, :].bitcast(U32).unsqueeze(1).broadcast_to([P, H, P])

            for gr, cs, t, turn, s in both_ways(dve, groups, new_state):
                for d in range(2):
                    dve.wait_ge(S["sums_mm"][d], t + 1)
                    nc.vector.tensor_copy(sm[:, d, :], ps[:, bank(d, 1), 0:2 * H]).then_inc(S["sums_copied"][d], 1)
                    dve.wait_ge(S["sums_copied"][d], t + 1)
                    dve.wait_ge(S["row_copied"][d], t + 1)
                    for dst, op, done in ((dn, ALU.max, S["below"]), (dt, ALU.min, S["above"])):
                        for h in range(H):
                            ins = nc.vector.tensor_scalar(head(dst[:, d, :], h), head(grow[:, d, :], h), sm[:, d, h:h + 1], 0.0, ALU.subtract, op)
                            own.mark(ins)
                        own.settle()
                        dve.sem_inc(done[d], 1)
                for d in range(2):
                    dve.wait_ge(S["sums_exp"][d], t + 1)
                    dve.wait_ge(chunk_in[d][s], (turn + 1) * 80)
                    b = ab_in[:, d, s, H:2 * H]
                    own.mark(nc.vector.tensor_tensor(fac[:, d, 0:H], b, esm[:, d, 0:H], ALU.mult))
                    own.mark(nc.vector.tensor_scalar(fac[:, d, H:2 * H], b, -1.0, None, ALU.mult))
                    own.mark(nc.vector.tensor_copy(by_head(T[:, d, :]), cst[:, IDENT, :].unsqueeze(1).broadcast_to([P, H, P])))
                    own.mark(nc.vector.tensor_copy(by_head(X[:, d, :]), cst[:, IDENT, :].unsqueeze(1).broadcast_to([P, H, P])))
                    own.settle()
                    dve.wait_ge(S["kk_mm"][d], t + 1)
                    dve.wait_ge(S["below_exp"][d], t + 1)
                    for h in range(H):
                        own.mark(nc.vector.scalar_tensor_tensor(head(neg_m[:, d, :], h), ps[:, bank(d, 0), h * P:(h + 1) * P],
                                                                fac[:, d, H + h:H + h + 1], head(dn[:, d, :], h), ALU.mult, ALU.mult))
                    own.settle()
                    dve.sem_inc(S["n_done"][d], 1)
                    dve.wait_ge(S["above_exp"][d], t + 1)
                    own.then(nc.vector.tensor_tensor(by_head(dt[:, d, :]), by_head(dt[:, d, :]),
                                                     cst[:, UPTO[d], :].unsqueeze(1).broadcast_to([P, H, P]), ALU.mult))
                    dve.wait_ge(S["qk_mm"][d], t + 1)
                    nc.vector.tensor_tensor(qk[:, d, :], ps[:, bank(d, 1), :], dt[:, d, :], ALU.mult).then_inc(S["qk_done"][d], 1)
                    dve.sem_inc(S["passed"], 1)
                    nc.vector.copy_predicated(by_head(T[:, d, :]), mask(PAIR[1 - d]), by_head(neg_m[:, d, :])).then_inc(S["t_placed"][d], 1)
                for d in range(2):
                    wait_alone(dve, S["turned_n"][d], t + 1, S["passed"])
                    nc.vector.copy_predicated(by_head(X[:, d, :]), mask(PAIR[d]), by_head(ps[:, bank(d, 1), :])).then_inc(S["x_placed"][d], 1)
                for d in range(2):
                    own.mark(nc.vector.tensor_tensor(by_head(kb[:, d, :]), by_head(k_in[:, d, s, :]), per_head(fac[:, d, 0:H]), ALU.mult))
                    own.mark(nc.vector.tensor_tensor(by_head(kd[:, d, :]), by_head(k_in[:, d, s, :]), per_head(esm[:, d, H:2 * H]), ALU.mult))
                    own.mark(nc.vector.tensor_tensor(by_head(vb[:, d, :]), by_head(v_in[:, d, s, :]), per_head(ab_in[:, d, s, H:2 * H]), ALU.mult))
                    own.settle()
                    dve.sem_inc(S["scaled"][d], 1)
                    dve.wait_ge(S["eg_done"][d], t + 1)
                    dve.wait_ge(S["copied"][d], 2 * t + 2)
                    nc.vector.tensor_tensor(qe[:, d, :], qT[:, d, :], eg[:, d, :], ALU.mult).then_inc(S["qe_done"][d], 1)
                for level in range(1, LEVELS):
                    for d in range(2):
                        if level < L:
                            dve.wait_ge(S["t_mm"][d], (L - 1) * t + level)
                        dve.wait_ge(S["x_placed"][d], LEVELS * t + level)
                        wait_alone(dve, S["x_mm"][d], L * t + level, S["passed"])
                        nc.vector.copy_predicated(by_head(X[:, d, :]), mask(PAIR[d] + level), by_head(ps[:, bank(d, 1), :])).then_inc(S["x_placed"][d], 1)
                        if level < L:
                            wait_alone(dve, S["t_placed"][d], L * t + level, S["passed"])
                            nc.vector.copy_predicated(by_head(T[:, d, :]), mask(PAIR[1 - d] + level), by_head(ps[:, bank(d, 0), :])).then_inc(S["t_placed"][d], 1)
                for d in range(2):
                    dve.wait_ge(S["v_mm"][d], t + 1)
                    nc.vector.tensor_copy(vn[:, d, :], ps[:, bank(d, 0), :]).then_inc(S["vn_done"][d], 1)
                for d in range(2):
                    wait_alone(dve, S["out_mm"][d], t + 1, S["passed"])
                    o = o_sb[:, bass.ds(cs[d], 1), bass.ds(gr * W, W)].rearrange("p a w -> p (a w)")
                    own.then(nc.vector.tensor_tensor(o, ps[:, bank(d, 2), :], o, ALU.add))
                    dve.sem_inc(S["out_done"][d], 1)
                    dve.wait_ge(S["state_mm"][d], t + 3)
                    last = P - 1 if d == 0 else 0
                    for h in range(H):
                        own.mark(nc.vector.scalar_tensor_tensor(head(state[:, d, :], h), head(state[:, d, :], h), eg[:, d, h * P + last:h * P + last + 1],
                                                                ps[:, bank(d, 1), h * P:(h + 1) * P], ALU.mult, ALU.add))
                    own.settle()
                    dve.sem_inc(S["state_done"][d], 1)
                own.restart()



GLA_HEADS, GLA_DK, GLA_DV, GLA_RANK, GLA_TAU = 4, 64, 128, 16, 16.0
ATT_HEADS, ATT_KV, ATT_DH = 8, 2, 64
E_Q, E_K = 0, GLA_HEADS * GLA_DK
E_V = 2 * GLA_HEADS * GLA_DK
E_OG = E_V + GLA_HEADS * GLA_DV
E_Z = E_OG + GLA_HEADS * GLA_DV
E_AQ = E_Z + 2 * GLA_RANK
E_AK = E_AQ + ATT_HEADS * ATT_DH
E_AV = E_AK + ATT_KV * ATT_DH
E_ALL = E_AV + ATT_KV * ATT_DH
O_V, O_OG = 3 * D, 4 * D


def row_tiles(eng):
    with eng.Fori(0, TILES // 2) as i:
        for s in range(2):
            yield 2 * i + s, i, s


def even_prep(nc, tag, proj, w_gate, b_gate, q_gain, k_gain, rope, cst, q, k, g, aq, ak):
    W = GLA_HEADS * P
    NH = ATT_HEADS + ATT_KV
    NG = GLA_HEADS * GLA_DK
    with contextlib.ExitStack() as stack:
        def sb(name, *shape):
            return stack.enter_context(nc.sbuf_tensor(f"{tag}_{name}", [P, *shape], F32))

        x = sb("x", 2, E_ALL)
        cs = sb("cs", 2, ATT_DH)
        wg = sb("wg", 2, NG)
        bias = sb("bias", 2 * NG)
        gain = sb("gain", NH, ATT_DH)
        zT = sb("zT", 2 * P)
        lx = sb("lx", 2 * NG)
        soft = sb("soft", 2 * NG)
        qp = sb("qp", 2, W)
        kp = sb("kp", 2, W)
        gp = sb("gp", 2, 2, W)
        sq = sb("sq", NH * ATT_DH)
        ss = sb("ss", 3, NH)
        n = sb("n", NH * ATT_DH)
        t0 = sb("t0", NH * ATT_DH)
        ro = sb("ro", 2, NH * ATT_DH)
        ps = stack.enter_context(nc.psum_tensor(f"{tag}_ps", [P, 2, 512], F32))
        block, S = stack.enter_context(phase(nc, tag, "tile_in*2", "const_in", "turned", "copied", "logits", "biased", "softened",
                                             "mean_done", "root_done", "tile_done", "stored*2", "own", "own_act"))

        @block.sync
        def _(sp):
            sp.dma_start(wg[0:GLA_RANK, :, :], w_gate.rearrange("d r n -> r d n")).then_inc(S["const_in"], 16)
            sp.dma_start(bias[:, :], over_partitions(b_gate.rearrange("d n -> (d n)"))).then_inc(S["const_in"], 16)
            for h in range(NH):
                sp.dma_start(gain[:, h, :], over_partitions(q_gain if h < ATT_HEADS else k_gain)).then_inc(S["const_in"], 16)
            for t, turn, s in row_tiles(sp):
                sp.wait_ge(S["tile_done"], t + 1)
                sp.dma_start(x[:, s, :], proj[bass.ts(t, P), :]).then_inc(S["tile_in"][s], 16)
                sp.dma_start(cs[:, s, :], rope[bass.ts(t, P), :]).then_inc(S["tile_in"][s], 16)

        @block.tensor
        def _(pe):
            pe.wait_ge(S["const_in"], 16 * (2 + NH))
            for t, turn, s in row_tiles(pe):
                pe.wait_ge(S["tile_in"][s], (turn + 1) * 32)
                pe.wait_ge(S["copied"], t + 1)
                for d in range(2):
                    z = x[:, s, E_Z + d * GLA_RANK:E_Z + (d + 1) * GLA_RANK]
                    mm = nc.tensor.transpose(ps[0:GLA_RANK, 0, d * P:(d + 1) * P], z, cst[:, IDENT, :])
                mm.then_inc(S["turned"], 1)
                pe.wait_ge(S["copied"], t + 2)
                pe.wait_ge(S["biased"], t + 1)
                for d in range(2):
                    mm = nc.tensor.matmul(ps[:, 1, d * NG:(d + 1) * NG], zT[0:GLA_RANK, d * P:(d + 1) * P], wg[0:GLA_RANK, d, :], start=True, stop=True)
                mm.then_inc(S["logits"], 1)

        @block.scalar
        def _(act):
            own = Steps(act, S["own_act"])
            act.sem_inc(S["copied"], 1)
            for s in range(2):
                act.sem_inc(S["stored"][s], 16)
            for t, turn, s in row_tiles(act):
                act.wait_ge(S["turned"], t + 1)
                nc.scalar.copy(zT[0:GLA_RANK, :], ps[0:GLA_RANK, 0, 0:2 * P]).then_inc(S["copied"], 1)
                act.wait_ge(S["biased"], t + 2)
                own.then(nc.scalar.activation(soft[:, :], lx[:, :], ACT.Abs))
                own.then(nc.scalar.activation(soft[:, :], soft[:, :], ACT.Exp, scale=-1.0))
                own.then(nc.scalar.activation(soft[:, :], soft[:, :], ACT.Ln, bias=1.0))
                act.sem_inc(S["softened"], 1)
                act.wait_ge(S["mean_done"], t + 1)
                nc.scalar.activation(ss[:, 2, :], ss[:, 1, :], ACT.Sqrt).then_inc(S["root_done"], 1)
                own.restart()
                act.wait_ge(S["tile_done"], t + 3)
                rows = bass.ts(t, P)
                for dst, src in ((q[rows, :], qp[:, s, :]), (k[rows, :], kp[:, s, :]), (g[0, rows, :], gp[:, s, 0, :]), (g[1, rows, :], gp[:, s, 1, :]),
                                 (aq[rows, :], ro[:, s, 0:ATT_HEADS * ATT_DH]), (ak[rows, :], ro[:, s, ATT_HEADS * ATT_DH:])):
                    act.dma_start(dst, src).then_inc(S["stored"][s], 16)
            for s in range(2):
                act.wait_ge(S["stored"][s], 16 + TILES // 2 * 96)

        @block.vector
        def _(dve):
            own = Steps(dve, S["own"])
            for pad in (qp, kp, gp):
                own.mark(nc.vector.memset(pad[:], 0.0))
            own.restart()
            dve.sem_inc(S["tile_done"], 2)
            dve.sem_inc(S["biased"], 1)
            dve.wait_ge(S["const_in"], 16 * (2 + NH))
            for t, turn, s in row_tiles(dve):
                dve.wait_ge(S["tile_in"][s], (turn + 1) * 32)
                dve.wait_ge(S["stored"][s], turn * 96 + 16)
                xs = x[:, s, :]

                def lower(x4):
                    return x4.rearrange("p (h f) -> p h f", f=P)[:, :, 0:GLA_DK]

                def by_head(x2):
                    return x2.rearrange("p (h f) -> p h f", f=GLA_DK)

                own.mark(nc.vector.tensor_scalar(lower(qp[:, s, :]), by_head(xs[:, E_Q:E_K]), GLA_DK ** -0.5, None, ALU.mult))
                own.mark(nc.vector.tensor_copy(lower(kp[:, s, :]), by_head(xs[:, E_K:E_V])))
                dve.wait_ge(S["logits"], t + 1)
                own.then(nc.vector.tensor_tensor(lx[:, :], ps[:, 1, :], bias[:, :], ALU.add))
                dve.sem_inc(S["biased"], 1)
                a = xs[:, E_AQ:E_AV]
                own.then(nc.vector.tensor_tensor(sq[:, :], a, a, ALU.mult))
                own.then(nc.vector.tensor_reduce(ss[:, 0, :], sq[:, :].rearrange("p (h f) -> p h f", h=NH), AX.X, ALU.add))
                nc.vector.tensor_scalar(ss[:, 1, :], ss[:, 0, :], 1.0 / ATT_DH, EPS, ALU.mult, ALU.add).then_inc(S["mean_done"], 1)
                dve.wait_ge(S["softened"], t + 1)
                own.then(nc.vector.scalar_tensor_tensor(soft[:, :], lx[:, :], 0.0, soft[:, :], ALU.min, ALU.subtract))
                for d in range(2):
                    own.mark(nc.vector.tensor_scalar(lower(gp[:, s, d, :]), by_head(soft[:, d * NG:(d + 1) * NG]), 1.0 / GLA_TAU, None, ALU.mult))
                dve.wait_ge(S["root_done"], t + 1)
                own.then(nc.vector.reciprocal(ss[:, 0, :], ss[:, 2, :]))
                n3 = n[:, :].rearrange("p (h f) -> p h f", h=NH)
                own.then(nc.vector.tensor_tensor(n3, a.rearrange("p (h f) -> p h f", h=NH), ss[:, 0, :].unsqueeze(2).broadcast_to([P, NH, ATT_DH]), ALU.mult))
                own.then(nc.vector.tensor_tensor(n3, n3, gain[:, :, :], ALU.mult))
                pairs = n[:, :].rearrange("p (h f two) -> p h f two", h=NH, two=2)
                cos, sin = (cs[:, s, j * ATT_DH // 2:(j + 1) * ATT_DH // 2].unsqueeze(1).broadcast_to([P, NH, ATT_DH // 2]) for j in range(2))
                tmp = t0[:, :].rearrange("p (two h f) -> p two h f", two=2, h=NH)
                sq2 = sq[:, :].rearrange("p (two h f) -> p two h f", two=2, h=NH)
                for j, (m0, m1, op) in enumerate(((cos, sin, ALU.subtract), (sin, cos, ALU.add))):
                    own.mark(nc.vector.tensor_tensor(tmp[:, j], pairs[:, :, :, 0], m0, ALU.mult))
                    own.mark(nc.vector.tensor_tensor(sq2[:, j], pairs[:, :, :, 1], m1, ALU.mult))
                own.settle()
                rot = ro[:, s, :].rearrange("p (h f two) -> p h f two", h=NH, two=2)
                for j, op in enumerate((ALU.subtract, ALU.add)):
                    own.mark(nc.vector.tensor_tensor(rot[:, :, :, j], tmp[:, j], sq2[:, j], op))
                own.restart()
                dve.sem_inc(S["tile_done"], 1)


def odd_prep(nc, tag, proj, bounds, q, k, g, room):
    X3 = 3 * D
    with contextlib.ExitStack() as stack:
        def sb(name, *shape):
            return stack.enter_context(nc.sbuf_tensor(f"{tag}_{name}", [P, *shape], F32))

        x = sb("x", 2, X3)
        sig = sb("sig", X3)
        off = sb("off", 2 * D)
        bnd = sb("bnd", 2, 2, D)
        top = sb("top", 2, D)
        lb = sb("lb", 2, D)
        rest = sb("rest", 2, D)
        qo = sb("qo", 2, D)
        ko = sb("ko", 2, 2 * D)
        go = room[:, 0:4, :].rearrange("p (s two) n -> p s (two n)", s=2)
        block, S = stack.enter_context(phase(nc, tag, "tile_in*2", "const_in", "bounds_top", "bounds_exp", "sigmoids", "sigmoids_used", "gates_done",
                                             "log_done", "tile_done", "stored*2", "own"))

        @block.sync
        def _(sp):
            sp.dma_start(bnd[:, :, :, :].rearrange("p d l n -> p (d l n)"), over_partitions(bounds.rearrange("d l n -> (d l n)"))).then_inc(S["const_in"], 16)
            for t, turn, s in row_tiles(sp):
                sp.wait_ge(S["tile_done"], t + 1)
                sp.dma_start(x[:, s, :], proj[bass.ts(t, P), 0:X3]).then_inc(S["tile_in"][s], 16)

        @block.scalar
        def _(act):
            act.wait_ge(S["bounds_top"], 1)
            nc.scalar.activation(bnd[:, :, :, :], bnd[:, :, :, :], ACT.Exp).then_inc(S["bounds_exp"], 1)
            for s in range(2):
                act.sem_inc(S["stored"][s], 16)
            for t, turn, s in row_tiles(act):
                act.wait_ge(S["tile_in"][s], (turn + 1) * 16)
                act.wait_ge(S["sigmoids_used"], t + 1)
                nc.scalar.activation(sig[:, :], x[:, s, :], ACT.Sigmoid).then_inc(S["sigmoids"], 1)
                nc.scalar.activation(off[:, :], x[:, s, D:], ACT.Sigmoid, scale=-1.0).then_inc(S["sigmoids"], 1)
                act.wait_ge(S["gates_done"], t + 1)
                nc.scalar.activation(go[:, s, :], go[:, s, :], ACT.Ln).then_inc(S["log_done"], 1)
                act.wait_ge(S["tile_done"], t + 3)
                act.wait_ge(S["log_done"], t + 1)
                rows = bass.ts(t, P)
                for dst, src in ((q[rows, :], qo[:, s, :]), (k[0, rows, :], ko[:, s, 0:D]), (k[1, rows, :], ko[:, s, D:]),
                                 (g[0, rows, :], go[:, s, 0:D]), (g[1, rows, :], go[:, s, D:])):
                    act.dma_start(dst, src).then_inc(S["stored"][s], 16)
            for s in range(2):
                act.wait_ge(S["stored"][s], 16 + TILES // 2 * 80)

        @block.vector
        def _(dve):
            own = Steps(dve, S["own"])
            dve.sem_inc(S["tile_done"], 2)
            dve.sem_inc(S["sigmoids_used"], 1)
            dve.wait_ge(S["const_in"], 16)
            own.then(nc.vector.tensor_tensor(top[:, :, :], bnd[:, :, 0, :], bnd[:, :, 1, :], ALU.max))
            for layer in range(2):
                own.mark(nc.vector.tensor_tensor(bnd[:, :, layer, :], bnd[:, :, layer, :], top[:, :, :], ALU.subtract))
            own.settle()
            dve.sem_inc(S["bounds_top"], 1)
            dve.wait_ge(S["bounds_exp"], 1)
            own.then(nc.vector.tensor_tensor(top[:, :, :], bnd[:, :, 0, :], bnd[:, :, 1, :], ALU.add))
            own.then(nc.vector.reciprocal(top[:, :, :], top[:, :, :]))
            for layer in range(2):
                own.mark(nc.vector.tensor_tensor(bnd[:, :, layer, :], bnd[:, :, layer, :], top[:, :, :], ALU.mult))
            own.settle()
            own.then(nc.vector.tensor_tensor(lb[:, :, :], bnd[:, :, 0, :], bnd[:, :, 1, :], ALU.add))
            own.then(nc.vector.tensor_tensor(lb[:, :, :], lb[:, :, :], bnd[:, :, 0, :], ALU.subtract))
            own.then(nc.vector.tensor_scalar(rest[:, :, :], lb[:, :, :], -1.0, 1.0, ALU.mult, ALU.add))
            own.restart()
            lb2 = lb[:, :, :].rearrange("p d n -> p (d n)")
            rest2 = rest[:, :, :].rearrange("p d n -> p (d n)")
            for t, turn, s in row_tiles(dve):
                dve.wait_ge(S["tile_in"][s], (turn + 1) * 16)
                dve.wait_ge(S["sigmoids"], 2 * t + 1)
                dve.wait_ge(S["stored"][s], turn * 80 + 16)
                own.then(nc.vector.tensor_tensor(go[:, s, :], sig[:, D:], rest2, ALU.mult))
                nc.vector.scalar_tensor_tensor(go[:, s, :], go[:, s, :], 1e-19, lb2, ALU.max, ALU.add).then_inc(S["gates_done"], 1)
                own.mark(nc.vector.tensor_tensor(qo[:, s, :], x[:, s, 0:D], sig[:, 0:D], ALU.mult))
                dve.wait_ge(S["sigmoids"], 2 * t + 2)
                own.then(nc.vector.tensor_tensor(ko[:, s, :], off[:, :], rest2, ALU.mult))
                dve.sem_inc(S["sigmoids_used"], 1)
                own.restart()
                dve.sem_inc(S["tile_done"], 1)


def gated_readout(nc, tag, o, heads, gates, gates_at, gain, tile0=0):
    W = heads * P
    tiles = TILES - tile0
    with contextlib.ExitStack() as stack:
        def sb(name, *shape):
            return stack.enter_context(nc.sbuf_tensor(f"{tag}_{name}", [P, *shape], F32))

        og = sb("og", 2, W)
        sq = sb("sq", 2, W)
        ss = sb("ss", 3, tiles * heads)
        gn = sb("gn", P)
        block, S = stack.enter_context(phase(nc, tag, "gates_in*2", "gain_in", "mean_done", "root_done", "silu_done", "tile_done", "own"))

        @block.sync
        def _(sp):
            sp.dma_start(gn[:, :], over_partitions(gain)).then_inc(S["gain_in"], 16)
            for n in range(tiles):
                if n >= 2:
                    sp.wait_ge(S["tile_done"], n - 1)
                sp.dma_start(og[:, n % 2, :], gates[(tile0 + n) * P:(tile0 + n + 1) * P, gates_at:gates_at + W]).then_inc(S["gates_in"][n % 2], 16)

        @block.scalar
        def _(act):
            act.wait_ge(S["mean_done"], 1)
            nc.scalar.activation(ss[:, 2, :], ss[:, 1, :], ACT.Sqrt).then_inc(S["root_done"], 1)
            for n in range(tiles):
                act.wait_ge(S["gates_in"][n % 2], (n // 2 + 1) * 16)
                nc.scalar.activation(og[:, n % 2, :], og[:, n % 2, :], ACT.Silu).then_inc(S["silu_done"], 1)

        @block.vector
        def _(dve):
            own = Steps(dve, S["own"])
            for n in range(tiles):
                a = o[:, tile0 + n, 0:W]
                own.mark(nc.vector.tensor_tensor(sq[:, n % 2, :], a, a, ALU.mult))
                own.settle()
                own.mark(nc.vector.tensor_reduce(ss[:, 0, n * heads:(n + 1) * heads], sq[:, n % 2, :].rearrange("p (h f) -> p h f", h=heads), AX.X, ALU.add))
            own.settle()
            nc.vector.tensor_scalar(ss[:, 1, :], ss[:, 0, :], 1.0 / P, EPS, ALU.mult, ALU.add).then_inc(S["mean_done"], 1)
            dve.wait_ge(S["root_done"], 1)
            own.then(nc.vector.reciprocal(ss[:, 0, :], ss[:, 2, :]))
            dve.wait_ge(S["gain_in"], 16)
            for n in range(tiles):
                a = o[:, tile0 + n, 0:W].rearrange("p (h f) -> p h f", h=heads)
                r = ss[:, 0, n * heads:(n + 1) * heads].unsqueeze(2).broadcast_to([P, heads, P])
                gate = og[:, n % 2, :].rearrange("p (h f) -> p h f", h=heads)
                own.mark(nc.vector.tensor_tensor(a, a, r, ALU.mult))
                dve.wait_ge(S["silu_done"], n + 1)
                own.then(nc.vector.tensor_tensor(gate, gate, gn[:, :].unsqueeze(1).broadcast_to([P, heads, P]), ALU.mult))
                nc.vector.tensor_tensor(a, a, gate, ALU.mult).then_inc(S["tile_done"], 1)


def turn_over(nc, tag, x, xT, ident, tile0=0, x_tile0=None):
    x0 = tile0 if x_tile0 is None else x_tile0
    with (
        nc.psum_tensor(f"{tag}_ps", [P, 4, 512], F32) as ps,
        phase(nc, tag, "turned", "taken_even", "taken_odd") as (block, S),
    ):
        jobs = [(t, half) for t in range(TILES - tile0) for half in range(2)]

        @block.tensor
        def _(pe):
            for n, (t, half) in enumerate(jobs):
                if n >= 4:
                    pe.wait_ge(S["taken_even"] if n % 2 == 0 else S["taken_odd"], (n - 4) // 2 + 1)
                for k in range(4):
                    mm = nc.tensor.transpose(ps[:, n % 4, k * P:(k + 1) * P], x[:, x0 + t, 4 * half + k::KD], ident)
                mm.then_inc(S["turned"], 1)

        def take(eng, copy, parity, done):
            for n, (t, half) in enumerate(jobs):
                if n % 2 == parity:
                    eng.wait_ge(S["turned"], n + 1)
                    copy(xT[:, 4 * half:4 * half + 4, (tile0 + t) * P:(tile0 + t + 1) * P],
                         ps[:, n % 4, :].rearrange("p (k t) -> p k t", k=4)).then_inc(done, 1)

        @block.vector
        def _(dve):
            take(dve, nc.vector.tensor_copy, 0, S["taken_even"])

        @block.scalar
        def _(act):
            take(act, nc.scalar.copy, 1, S["taken_odd"])




def load_tiles(nc, tag, *pairs):
    with phase(nc, tag, "loaded") as (block, S):
        @block.sync
        def _(sp):
            for dst, src in pairs:
                sp.dma_start(dst, src).then_inc(S["loaded"], 16)
            sp.wait_ge(S["loaded"], 16 * len(pairs))


def first_block(nc, I, x, hT, mix, cst, ident):
    even_proj = nc.dram_tensor("even_proj", (N_TOK, E_ALL), F32).ap()
    odd_proj = nc.dram_tensor("odd_proj", (N_TOK, 5 * D), F32).ap()
    gla_q, gla_k = (nc.dram_tensor(f"gla_{n}", (N_TOK, GLA_HEADS * P), F32).ap() for n in "qk")
    gla_g = nc.dram_tensor("gla_g", (2, N_TOK, GLA_HEADS * P), F32).ap()
    att_q = nc.dram_tensor("att_q", (N_TOK, ATT_HEADS * ATT_DH), F32).ap()
    att_k = nc.dram_tensor("att_k", (N_TOK, ATT_KV * ATT_DH), F32).ap()
    hg_q = nc.dram_tensor("hgrn_q", (N_TOK, D), F32).ap()
    hg_k, hg_g = (nc.dram_tensor(f"hgrn_{n}", (2, N_TOK, D), F32).ap() for n in "kg")
    mods = [nc.dram_tensor(f"mod{layer}", (2, 6 * D), F32).ap() for layer in range(2)]
    for layer in range(2):
        modulation(nc, f"mod{layer}", I["c"][0], I["c_ctx"], I["mod_w"][layer], I["mod_b"][layer], mods[layer])
    load_tiles(nc, "start", (cst[:, :, :], I["tables"]),
               (x[:, 0:CTX_TILES, :], I["ctx"][0].rearrange("(m p) d -> p m d", p=P)),
               (x[:, CTX_TILES:, :], I["x"][0].rearrange("(m p) d -> p m d", p=P)))
    y = hT[:, :, :].rearrange("p k t -> p (k t)").rearrange("p (m d) -> p m d", d=D)

    modulated_norm(nc, "n0", x, hT, ident, I["norm_pre_mix"][0], mods[0], 0, 1)
    linear(nc, "in0", hT, KD, I["even_w_in"][0], TILES, out=even_proj)
    even_prep(nc, "prep0", even_proj, I["gla_w_gate"][0], I["gla_b_gate"][0], I["att_q_norm"][0], I["att_k_norm"][0],
              I["rope_pairs"], cst, gla_q, gla_k, gla_g, att_q, att_k)
    for d in range(2):
        gated_scan(nc, f"gla{d}", d, 1, gla_q, gla_k, gla_g[d], even_proj, E_V, mix, cst)
    gated_readout(nc, "ro0", mix, GLA_HEADS, even_proj, E_OG, I["gla_out_norm"][0])
    attention(nc, "att0", att_q, att_k, even_proj, mix, GLA_HEADS * P, ident, ATT_HEADS, ATT_HEADS // ATT_KV, ATT_DH, ATT_DH, ATT_DH, E_AV)
    turn_over(nc, "t0", mix, hT, ident)
    linear(nc, "out0", hT, KD, I["even_w_out"][0], TILES, out_sb=mix)
    gated_residual(nc, "res0", x, mix, mods[0], 2, I["norm_post_mix"][0])
    feed_forward(nc, "ffn0", x, hT, ident, I["norm_pre_ffn"][0], I["norm_post_ffn"][0], mods[0],
                 I["ffn_w_gate"][0], I["ffn_w_up"][0], I["ffn_w_down"][0], 0)

    modulated_norm(nc, "n1", x, hT, ident, I["norm_pre_mix"][1], mods[1], 0, 1)
    linear(nc, "in1", hT, KD, I["odd_w_in"][0], TILES, out=odd_proj)
    odd_prep(nc, "prep1", odd_proj, I["hgrn_lower_bounds"], hg_q, hg_k, hg_g, mix)
    for d in range(2):
        gated_scan(nc, f"hgrn{d}", d, 2, hg_q, hg_k[d], hg_g[d], odd_proj, O_V, mix, cst)
    gated_readout(nc, "ro1", mix, 8, odd_proj, O_OG, I["hgrn_out_norm"][0], CTX_TILES)
    turn_over(nc, "t1", mix, hT, ident, CTX_TILES)
    linear(nc, "out1", hT, KD, I["odd_w_out"][0], TILES - CTX_TILES, CTX_TILES, out_sb=mix)
    gated_residual(nc, "res1", x, mix, mods[1], 2, I["norm_post_mix"][1], CTX_TILES)
    feed_forward(nc, "ffn1", x, hT, ident, I["norm_pre_ffn"][1], I["norm_post_ffn"][1], mods[1],
                 I["ffn_w_gate"][1], I["ffn_w_up"][1], I["ffn_w_down"][1], CTX_TILES)


def rope_pairs():
    import numpy as np

    half = ATT_DH // 2
    inv = np.float32(10000.0) ** (-np.arange(0, half, 2, dtype=np.float32) / np.float32(half))
    row, col = np.divmod(np.arange(LAT), 64)
    ang = np.concatenate([row.astype(np.float32)[:, None] * inv, col.astype(np.float32)[:, None] * inv], -1)
    still = np.concatenate([np.ones((CTX, half)), np.zeros((CTX, half))], -1)
    return np.concatenate([still, np.concatenate([np.cos(ang), np.sin(ang)], -1)]).astype(np.float32)



DN_HEADS, DN_CONV = 8, 5
QKV = 3 * D
MLA_HEADS, Q_RANK, KV_RANK, NOPE, ROPE, MLA_DV = 8, 384, 256, 128, 64, 128
MLA_DH = NOPE + ROPE
S_Z = 0
S_ALPHA = S_Z + D
S_BETA = S_ALPHA + 2 * DN_HEADS
S_CQ = S_BETA + 2 * DN_HEADS
S_CKV = S_CQ + Q_RANK
S_KROPE = S_CKV + KV_RANK
S_GATE = S_KROPE + ROPE
S_ALL = S_GATE + 2 * D
EXPERTS, EXPERT_FF = 16, 1408
SLOTS = 2 * LAT // EXPERTS


def conv_projection(nc, tag, hT, w, taps, out, ident):
    width = 512
    f_tiles = width // P
    pad = DN_CONV // 2
    starts = (pad, 3 * pad + CTX)
    row = CTX + LAT + 4 * pad
    span = row - 2 * pad
    blocks = QKV // width
    w_v = w.rearrange("(p k) n -> p k n", p=P)
    segments = ((0, CTX), (CTX, LAT))
    with contextlib.ExitStack() as stack:
        def sb(name, *shape):
            return stack.enter_context(nc.sbuf_tensor(f"{tag}_{name}", [P, *shape], F32))

        wt = sb("w", 2, KD, width)
        tp = sb("taps", DN_CONV, QKV // P)
        raw = sb("raw", 2, row)
        acc = sb("acc", 2, span)
        turned = sb("turned", 2, TILES, P)
        ps = stack.enter_context(nc.psum_tensor(f"{tag}_ps", [P, 8, 512], F32))
        block, S = stack.enter_context(phase(nc, tag, "w_in*2", "taps_in", "w_used", "mm_done", "padded", "conv_done", "silu_done",
                                             "turned_mm", "taken", "stored*2", "own"))
        out_v = out.rearrange("(m p) c -> p m c", p=P)

        def f_of(eng):
            with eng.Fori(0, blocks // 2) as i:
                for s in range(2):
                    for f in range(f_tiles):
                        yield (2 * i + s) * f_tiles + f, f, 2 * i + s, s, i

        @block.sync
        def _(sp):
            for j in range(DN_CONV):
                sp.dma_start(tp[:, j, :], taps[j].rearrange("(f p) -> p f", p=P), allow_slow_non_contiguous=True).then_inc(S["taps_in"], 16)
            for b, s, turn, wd in blocks_of(sp, QKV, width):
                sp.wait_ge(S["w_used"], b + 1)
                sp.dma_start(wt[:, s, :, :], w_v[:, :, bass.ds(b * width, width)]).then_inc(S["w_in"][s], 16)

        @block.tensor
        def _(pe):
            pe.sem_inc(S["w_used"], 2)

            def turn(n, f):
                pe.wait_ge(S["silu_done"], n + 1)
                for seg, (t0, t1) in enumerate(((0, 3), (3, 6))):
                    pe.wait_ge(S["taken"], 2 * n + seg + 1)
                    for t in range(t0, t1):
                        at = t * P if t < CTX_TILES else t * P + 2 * pad
                        mm = nc.tensor.transpose(ps[:, 4 + seg, (t - t0) * P:(t - t0 + 1) * P], acc[:, f % 2, at:at + P], ident)
                    mm.then_inc(S["turned_mm"], 1)

            per_turn = 2 * f_tiles
            with pe.Fori(0, blocks // 2) as i:
                for m in range(per_turn + 1):
                    n, f, s = i * per_turn + m, m % f_tiles, m // f_tiles
                    if m < per_turn:
                        if f == 0:
                            pe.wait_ge(S["w_in"][s], (i + 1) * 16)
                        pe.wait_ge(S["padded"], 2 * n + 2)
                        for seg, (t0, size) in enumerate(segments):
                            for k in range(KD):
                                mm = nc.tensor.matmul(ps[:, 2 * (f % 2) + seg, 0:size], wt[:, s, k, f * P:(f + 1) * P], hT[:, k, t0:t0 + size],
                                                      start=k == 0, stop=k == KD - 1)
                            mm.then_inc(S["mm_done"], 1)
                        if f == f_tiles - 1:
                            pe.wait_ge(S["mm_done"], 2 * n + 2)
                            pe.sem_inc(S["w_used"], 1)
                    if m:
                        turn(n - 1, (m - 1) % f_tiles)

        @block.scalar
        def _(act):
            act.sem_inc(S["padded"], 4)
            for s in range(2):
                act.sem_inc(S["stored"][s], 16)
            for n, f, b, s, i in f_of(act):
                act.wait_ge(S["conv_done"], n + 1)
                for seg, (t0, size) in enumerate(segments):
                    act.wait_ge(S["mm_done"], 2 * n + seg + 1)
                    nc.scalar.copy(raw[:, f % 2, starts[seg]:starts[seg] + size], ps[:, 2 * (f % 2) + seg, 0:size]).then_inc(S["padded"], 1)
                act.wait_ge(S["conv_done"], n + 3)
                nc.scalar.activation(acc[:, f % 2, :], acc[:, f % 2, :], ACT.Silu).then_inc(S["silu_done"], 1)
                act.wait_ge(S["taken"], 2 * n + 4)
                act.dma_start(out_v[:, :, bass.ts(n, P)], turned[:, f % 2, :, :]).then_inc(S["stored"][f % 2], 16)
            for s in range(2):
                act.wait_ge(S["stored"][s], 16 + QKV // P // 2 * 16)

        @block.vector
        def _(dve):
            own = Steps(dve, S["own"])
            own.mark(nc.vector.memset(raw[:, :, :], 0.0))
            own.restart()
            dve.sem_inc(S["conv_done"], 2)
            dve.sem_inc(S["taken"], 2)
            dve.wait_ge(S["taps_in"], 16 * DN_CONV)
            for n, f, b, s, i in f_of(dve):
                dve.wait_ge(S["padded"], 2 * n + 6)
                y = acc[:, f % 2, :]
                dve.wait_ge(S["taken"], 2 * n + 1)
                own.then(nc.vector.tensor_scalar(y, raw[:, f % 2, 0:span], tp[:, 0, bass.ds(n, 1)], None, ALU.mult))
                for j in range(1, DN_CONV):
                    own.then(nc.vector.scalar_tensor_tensor(y, raw[:, f % 2, j:j + span], tp[:, j, bass.ds(n, 1)], y, ALU.mult, ALU.add))
                own.restart()
                dve.sem_inc(S["conv_done"], 1)
                dve.wait_ge(S["stored"][f % 2], (2 * b + f // 2) * 16 + 16)
                for seg in range(2):
                    dve.wait_ge(S["turned_mm"], 2 * n + seg + 1)
                    nc.vector.tensor_copy(turned[:, f % 2, 3 * seg:3 * seg + 3, :].rearrange("p t c -> p (t c)"), ps[:, 4 + seg, 0:3 * P]).then_inc(S["taken"], 1)


def delta_prep(nc, tag, qkv, proj, a_log, dt_bias, q, k, decay, beta):
    NH = 2 * DN_HEADS
    with contextlib.ExitStack() as stack:
        def sb(name, *shape):
            return stack.enter_context(nc.sbuf_tensor(f"{tag}_{name}", [P, *shape], F32))

        x = sb("x", 2, NH, P)
        ab = sb("ab", 2, 2 * NH)
        al = sb("al", NH)
        dtb = sb("dtb", NH)
        sq = sb("sq", NH, P)
        ss = sb("ss", 3, NH)
        qk = sb("qk", 2, NH, P)
        lx = sb("lx", 2, NH)
        gb = sb("gb", 2, 2, NH)
        block, S = stack.enter_context(phase(nc, tag, "tile_in*2", "const_in", "rate_done", "sum_done", "root_done", "biased", "soft_done",
                                             "tile_done", "stored*2", "own", "own_act"))

        @block.sync
        def _(sp):
            sp.dma_start(al[:, :], over_partitions(a_log.rearrange("d h -> (d h)"))).then_inc(S["const_in"], 16)
            sp.dma_start(dtb[:, :], over_partitions(dt_bias.rearrange("d h -> (d h)"))).then_inc(S["const_in"], 16)
            for t, turn, s in row_tiles(sp):
                sp.wait_ge(S["tile_done"], t + 1)
                sp.dma_start(x[:, s, :, :].rearrange("p h f -> p (h f)"), qkv[bass.ts(t, P), 0:NH * P]).then_inc(S["tile_in"][s], 16)
                sp.dma_start(ab[:, s, :], proj[bass.ts(t, P), S_ALPHA:S_CQ]).then_inc(S["tile_in"][s], 16)

        @block.scalar
        def _(act):
            own = Steps(act, S["own_act"])
            act.wait_ge(S["const_in"], 32)
            nc.scalar.activation(al[:, :], al[:, :], ACT.Exp).then_inc(S["rate_done"], 1)
            for s in range(2):
                act.sem_inc(S["stored"][s], 16)
            for t, turn, s in row_tiles(act):
                act.wait_ge(S["biased"], t + 1)
                own.mark(nc.scalar.activation(gb[:, s, 1, :], ab[:, s, NH:], ACT.Exp, scale=-1.0))
                own.then(nc.scalar.activation(lx[:, 1, :], lx[:, 0, :], ACT.Abs))
                own.then(nc.scalar.activation(lx[:, 1, :], lx[:, 1, :], ACT.Exp, scale=-1.0))
                own.then(nc.scalar.activation(lx[:, 1, :], lx[:, 1, :], ACT.Ln, bias=1.0))
                act.sem_inc(S["soft_done"], 1)
                own.restart()
                act.wait_ge(S["sum_done"], t + 1)
                nc.scalar.activation(ss[:, 2, :], ss[:, 1, :], ACT.Sqrt).then_inc(S["root_done"], 1)
                act.wait_ge(S["tile_done"], t + 3)
                rows = bass.ts(t, P)
                for dst, src in ((q[rows, :], qk[:, s, 0:DN_HEADS, :].rearrange("p h f -> p (h f)")), (k[rows, :], qk[:, s, DN_HEADS:, :].rearrange("p h f -> p (h f)")),
                                 (decay[rows, :], gb[:, s, 0, :]), (beta[rows, :], gb[:, s, 1, :])):
                    act.dma_start(dst, src).then_inc(S["stored"][s], 16)
            for s in range(2):
                act.wait_ge(S["stored"][s], 16 + TILES // 2 * 64)

        @block.vector
        def _(dve):
            own = Steps(dve, S["own"])
            dve.sem_inc(S["tile_done"], 2)
            dve.wait_ge(S["rate_done"], 1)
            for t, turn, s in row_tiles(dve):
                dve.wait_ge(S["tile_in"][s], (turn + 1) * 32)
                dve.wait_ge(S["stored"][s], turn * 64 + 16)
                nc.vector.tensor_tensor(lx[:, 0, :], ab[:, s, 0:NH], dtb[:, :], ALU.add).then_inc(S["biased"], 1)
                a = x[:, s, :, :]
                own.then(nc.vector.tensor_tensor(sq[:, :, :], a, a, ALU.mult))
                own.then(nc.vector.tensor_reduce(ss[:, 0, :], sq[:, :, :], AX.X, ALU.add))
                nc.vector.tensor_scalar(ss[:, 1, :], ss[:, 0, :], EPS, None, ALU.add).then_inc(S["sum_done"], 1)
                dve.wait_ge(S["soft_done"], t + 1)
                own.mark(nc.vector.tensor_scalar(gb[:, s, 1, :], gb[:, s, 1, :], 1.0, None, ALU.add))
                own.then(nc.vector.scalar_tensor_tensor(lx[:, 1, :], lx[:, 0, :], 0.0, lx[:, 1, :], ALU.max, ALU.add))
                own.mark(nc.vector.scalar_tensor_tensor(gb[:, s, 0, :], lx[:, 1, :], -1.0, al[:, :], ALU.mult, ALU.mult))
                own.mark(nc.vector.reciprocal(gb[:, s, 1, :], gb[:, s, 1, :]))
                dve.wait_ge(S["root_done"], t + 1)
                own.then(nc.vector.reciprocal(ss[:, 0, :], ss[:, 2, :]))
                own.then(nc.vector.tensor_scalar(ss[:, 0, 0:DN_HEADS], ss[:, 0, 0:DN_HEADS], P ** -0.5, None, ALU.mult))
                own.mark(nc.vector.tensor_tensor(qk[:, s, :, :], a, ss[:, 0, :].unsqueeze(2).broadcast_to([P, NH, P]), ALU.mult))
                own.restart()
                dve.sem_inc(S["tile_done"], 1)


def latent_norm(nc, tag, src, gain, outT, ident, tile0=0):
    rank = src.shape[1]
    kt = rank // P
    tiles = list(range(tile0, TILES))
    with contextlib.ExitStack() as stack:
        def sb(name, *shape):
            return stack.enter_context(nc.sbuf_tensor(f"{tag}_{name}", [P, *shape], F32))

        x = sb("x", TILES, rank)
        sq = sb("sq", rank)
        gn = sb("gn", kt)
        ss = sb("ss", 3, TILES)
        ps = stack.enter_context(nc.psum_tensor(f"{tag}_ps", [P, 2, 512], F32))
        block, S = stack.enter_context(phase(nc, tag, "loaded", "squares", "mean_done", "root_done", "normed", "turned", "taken", "own_act", "own"))

        @block.sync
        def _(sp):
            sp.dma_start(x[:, tile0:, :], src.rearrange("(m p) c -> p m c", p=P)[:, tile0:, :]).then_inc(S["loaded"], 16)
            sp.dma_start(gn[:, :], gain.rearrange("(p k) -> p k", p=P)).then_inc(S["loaded"], 16)

        @block.scalar
        def _(act):
            own = Steps(act, S["own_act"])
            act.wait_ge(S["loaded"], 32)
            for t in tiles:
                own.then(nc.scalar.activation(sq[:, :], x[:, t, :], ACT.Square, accum_out=ss[:, 0, t:t + 1]))
            act.sem_inc(S["squares"], 1)
            act.wait_ge(S["mean_done"], 1)
            nc.scalar.activation(ss[:, 2, tile0:], ss[:, 1, tile0:], ACT.Sqrt).then_inc(S["root_done"], 1)
            for n, t in enumerate(tiles):
                act.wait_ge(S["turned"], n + 1)
                for k in range(kt):
                    own.mark(nc.scalar.activation(outT[:, k, t * P:(t + 1) * P], ps[:, n % 2, k * P:(k + 1) * P], ACT.Copy, scale=gn[:, k:k + 1]))
                own.settle()
                act.sem_inc(S["taken"], 1)

        @block.vector
        def _(dve):
            own = Steps(dve, S["own"])
            dve.wait_ge(S["squares"], 1)
            nc.vector.tensor_scalar(ss[:, 1, tile0:], ss[:, 0, tile0:], 1.0 / rank, EPS, ALU.mult, ALU.add).then_inc(S["mean_done"], 1)
            dve.wait_ge(S["root_done"], 1)
            own.then(nc.vector.reciprocal(ss[:, 0, tile0:], ss[:, 2, tile0:]))
            for t in tiles:
                nc.vector.tensor_scalar(x[:, t, :], x[:, t, :], ss[:, 0, t:t + 1], None, ALU.mult).then_inc(S["normed"], 1)

        @block.tensor
        def _(pe):
            for n, t in enumerate(tiles):
                pe.wait_ge(S["normed"], n + 1)
                if n >= 2:
                    pe.wait_ge(S["taken"], n - 1)
                for k in range(kt):
                    mm = nc.tensor.transpose(ps[:, n % 2, k * P:(k + 1) * P], x[:, t, k::kt], ident)
                mm.then_inc(S["turned"], 1)


def head_prep(nc, tag, parts, gain, rope, out, tile0=0):
    H, W = MLA_HEADS, MLA_HEADS * MLA_DH
    Q4 = ROPE // 4
    with contextlib.ExitStack() as stack:
        def sb(name, *shape):
            return stack.enter_context(nc.sbuf_tensor(f"{tag}_{name}", [P, *shape], F32))

        x = sb("x", 2, H, MLA_DH)
        cs = sb("cs", 2, 2 * ROPE)
        gn = sb("gn", MLA_DH)
        sq = sb("sq", H, MLA_DH)
        ss = sb("ss", 3, H)
        y = sb("y", 2, H, MLA_DH)
        t0 = sb("t0", H, ROPE)
        block, S = stack.enter_context(phase(nc, tag, "tile_in*2", "const_in", "mean_done", "root_done", "tile_done", "stored*2", "own"))
        loads = len(parts) + 1

        def tiles_of(eng):
            with eng.Fori(0, (TILES - tile0) // 2) as i:
                for s in range(2):
                    yield 2 * i + s, i, s

        @block.sync
        def _(sp):
            sp.dma_start(gn[:, :], over_partitions(gain)).then_inc(S["const_in"], 16)
            for n, turn, s in tiles_of(sp):
                sp.wait_ge(S["tile_done"], n + 1)
                for a, b, source in parts:
                    sp.dma_start(x[:, s, :, a:b], source(bass.ts(n + tile0, P))).then_inc(S["tile_in"][s], 16)
                sp.dma_start(cs[:, s, :], rope[bass.ts(n + tile0, P), :]).then_inc(S["tile_in"][s], 16)

        @block.scalar
        def _(act):
            for s in range(2):
                act.sem_inc(S["stored"][s], 16)
            for n, turn, s in tiles_of(act):
                act.wait_ge(S["mean_done"], n + 1)
                nc.scalar.activation(ss[:, 2, :], ss[:, 1, :], ACT.Sqrt).then_inc(S["root_done"], 1)
                act.wait_ge(S["tile_done"], n + 3)
                act.dma_start(out[bass.ts(n + tile0, P), :], y[:, s, :, :].rearrange("p h f -> p (h f)")).then_inc(S["stored"][s], 16)
            for s in range(2):
                act.wait_ge(S["stored"][s], 16 + (TILES - tile0) // 2 * 16)

        @block.vector
        def _(dve):
            own = Steps(dve, S["own"])
            dve.sem_inc(S["tile_done"], 2)
            dve.wait_ge(S["const_in"], 16)
            for n, turn, s in tiles_of(dve):
                dve.wait_ge(S["tile_in"][s], (turn + 1) * 16 * loads)
                a = x[:, s, :, :]
                own.then(nc.vector.tensor_tensor(sq[:, :, :], a, a, ALU.mult))
                own.then(nc.vector.tensor_reduce(ss[:, 0, :], sq[:, :, :], AX.X, ALU.add))
                nc.vector.tensor_scalar(ss[:, 1, :], ss[:, 0, :], 1.0 / MLA_DH, EPS, ALU.mult, ALU.add).then_inc(S["mean_done"], 1)
                dve.wait_ge(S["root_done"], n + 1)
                own.then(nc.vector.reciprocal(ss[:, 0, :], ss[:, 2, :]))
                own.then(nc.vector.tensor_tensor(a, a, ss[:, 0, :].unsqueeze(2).broadcast_to([P, H, MLA_DH]), ALU.mult))
                dve.wait_ge(S["stored"][s], turn * 16 + 16)
                own.then(nc.vector.tensor_tensor(y[:, s, :, :], a, gn[:, :].unsqueeze(1).broadcast_to([P, H, MLA_DH]), ALU.mult))
                pe_ = y[:, s, :, NOPE:]
                quarters = pe_.rearrange("p h (a b f) -> p h a b f", a=2, b=2)
                tmp = t0[:, :, :].rearrange("p h (a b f) -> p h a b f", a=2, b=2)
                sin = cs[:, s, ROPE:].rearrange("p (a b f) -> p a b f", a=2, b=2)
                for b in range(2):
                    own.mark(nc.vector.tensor_tensor(tmp[:, :, :, b, :], quarters[:, :, :, 1 - b, :],
                                                     sin[:, :, b, :].unsqueeze(1).broadcast_to([P, H, 2, Q4]), ALU.mult))
                own.settle()
                own.then(nc.vector.tensor_tensor(pe_, pe_, cs[:, s, 0:ROPE].unsqueeze(1).broadcast_to([P, H, ROPE]), ALU.mult))
                own.mark(nc.vector.tensor_tensor(pe_, pe_, t0[:, :, :], ALU.add))
                own.restart()
                dve.sem_inc(S["tile_done"], 1)


def merge(nc, tag, a, b, logits, logits_at):
    tiles = TILES - CTX_TILES
    with (
        nc.sbuf_tensor(f"{tag}_g", [P, 2, 2 * D], F32) as g,
        phase(nc, tag, "gates_in*2", "exp_done", "tile_done", "own") as (block, S),
    ):
        @block.sync
        def _(sp):
            for n in range(tiles):
                if n >= 2:
                    sp.wait_ge(S["tile_done"], n - 1)
                rows = slice((CTX_TILES + n) * P, (CTX_TILES + n + 1) * P)
                sp.dma_start(g[:, n % 2, :], logits[rows, logits_at:logits_at + 2 * D]).then_inc(S["gates_in"][n % 2], 16)

        @block.scalar
        def _(act):
            for n in range(tiles):
                act.wait_ge(S["gates_in"][n % 2], (n // 2 + 1) * 16)
                nc.scalar.activation(g[:, n % 2, :], g[:, n % 2, :], ACT.Sigmoid).then_inc(S["exp_done"], 1)

        @block.vector
        def _(dve):
            own = Steps(dve, S["own"])
            for n in range(tiles):
                dve.wait_ge(S["exp_done"], n + 1)
                own.mark(nc.vector.tensor_tensor(a[:, n, :], a[:, n, :], g[:, n % 2, 0:D], ALU.mult))
                own.mark(nc.vector.tensor_tensor(b[:, n, :], b[:, n, :], g[:, n % 2, D:], ALU.mult))
                own.settle()
                own.mark(nc.vector.tensor_tensor(a[:, n, :], a[:, n, :], b[:, n, :], ALU.add))
                dve.sem_inc(S["tile_done"], 1)
            own.settle()


def rope_quarters():
    import numpy as np

    n_freq = ROPE // 4
    inv = np.float32(10000.0) ** (-np.arange(n_freq, dtype=np.float32) / np.float32(n_freq))
    row, col = np.divmod(np.arange(LAT), 64)
    r, c = row.astype(np.float32)[:, None] * inv, col.astype(np.float32)[:, None] * inv
    ang = np.concatenate([r, r, c, c], -1)
    sign = np.repeat(np.array([-1, 1, -1, 1], np.float32), n_freq)
    still = np.concatenate([np.ones((CTX, ROPE)), np.zeros((CTX, ROPE))], -1)
    return np.concatenate([still, np.concatenate([np.cos(ang), np.sin(ang) * sign], -1)]).astype(np.float32)




def route(nc, tag, hT, router_w, cst, ones, slot_iota, pick, pick_gateT):
    tiles = TILES - CTX_TILES
    E = EXPERTS
    with contextlib.ExitStack() as stack:
        def sb(name, *shape):
            return stack.enter_context(nc.sbuf_tensor(f"{tag}_{name}", [P, *shape], F32))

        w = sb("w", KD, E)
        aff = sb("aff", tiles, E)
        red = sb("red", 4, tiles)
        affT = sb("affT", LAT)
        work = sb("work", LAT)
        top = sb("top", 8)
        taken = sb("taken", tiles, E)
        slot = sb("slot", tiles, E)
        gated = sb("gated", 2, E * SLOTS)
        ps = stack.enter_context(nc.psum_tensor(f"{tag}_ps", [P, 8, 512], F32))
        block, S = stack.enter_context(phase(nc, tag, "w_in", "logits", "max_done", "exp_done", "aff_done", "aff_turned", "mask_done", "mask_turned",
                                             "mask_back", "ranked", "gated_done", "pick_turned", "pick_even", "pick_odd", "own"))
        n_jobs = tiles * 2

        @block.sync
        def _(sp):
            sp.dma_start(w[:, :, :], router_w.rearrange("(p k) e -> p k e", p=P)).then_inc(S["w_in"], 16)

        @block.tensor
        def _(pe):
            pe.wait_ge(S["w_in"], 16)
            for m in range(tiles):
                for k in range(KD):
                    mm = nc.tensor.matmul(ps[:, 0, m * E:(m + 1) * E], hT[:, k, (CTX_TILES + m) * P:(CTX_TILES + m + 1) * P], w[:, k, :],
                                          start=k == 0, stop=k == KD - 1)
            mm.then_inc(S["logits"], 1)
            pe.wait_ge(S["aff_done"], 1)
            for m in range(tiles):
                mm = nc.tensor.transpose(ps[0:E, 1, m * P:(m + 1) * P], aff[:, m, :], cst[:, IDENT, :])
            mm.then_inc(S["aff_turned"], 1)
            pe.wait_ge(S["mask_done"], 1)
            for m in range(tiles):
                mm = nc.tensor.transpose(ps[:, 2, m * E:(m + 1) * E], work[0:E, m * P:(m + 1) * P], cst[0:E, IDENT, 0:E])
            mm.then_inc(S["mask_turned"], 1)
            pe.wait_ge(S["mask_back"], 1)
            for m in range(tiles):
                for before in range(m + 1):
                    mm = nc.tensor.matmul(ps[:, 3, m * E:(m + 1) * E], cst[:, UPTO[0], :] if before == m else ones, taken[:, before, :],
                                          start=before == 0, stop=before == m)
            mm.then_inc(S["ranked"], 1)
            for n in range(n_jobs):
                m, half = divmod(n, 2)
                pe.wait_ge(S["gated_done"], m + 1)
                if n >= 2:
                    pe.wait_ge(S["pick_even"] if n % 2 == 0 else S["pick_odd"], n // 2)
                for j in range(4):
                    pair = 4 * half + j
                    mm = nc.tensor.transpose(ps[:, 4 + n % 2, j * P:(j + 1) * P], gated[:, m % 2, pair * P:(pair + 1) * P], cst[:, IDENT, :])
                mm.then_inc(S["pick_turned"], 1)

        def take(eng, copy, n, done):
            m, half = divmod(n, 2)
            eng.wait_ge(S["pick_turned"], n + 1)
            copy(pick_gateT[:, 4 * half:4 * half + 4, m * P:(m + 1) * P], ps[:, 4 + n % 2, :].rearrange("p (j t) -> p j t", j=4)).then_inc(done, 1)

        @block.scalar
        def _(act):
            act.wait_ge(S["max_done"], 1)
            nc.scalar.activation(aff[:, :, :], aff[:, :, :], ACT.Exp).then_inc(S["exp_done"], 1)
            for n in range(1, n_jobs, 2):
                take(act, nc.scalar.copy, n, S["pick_odd"])

        @block.vector
        def _(dve):
            own = Steps(dve, S["own"])

            def over_experts(x):
                return x.unsqueeze(2).broadcast_to([P, tiles, E])

            dve.wait_ge(S["logits"], 1)
            lg = ps[:, 0, 0:tiles * E].rearrange("p (m e) -> p m e", m=tiles)
            own.then(nc.vector.tensor_reduce(red[:, 0, :], lg, AX.X, ALU.max))
            nc.vector.tensor_tensor(aff[:, :, :], lg, over_experts(red[:, 0, :]), ALU.subtract).then_inc(S["max_done"], 1)
            dve.wait_ge(S["exp_done"], 1)
            own.then(nc.vector.tensor_reduce(red[:, 1, :], aff[:, :, :], AX.X, ALU.add))
            own.then(nc.vector.reciprocal(red[:, 2, :], red[:, 1, :]))
            nc.vector.tensor_tensor(aff[:, :, :], aff[:, :, :], over_experts(red[:, 2, :]), ALU.mult).then_inc(S["aff_done"], 1)
            dve.wait_ge(S["aff_turned"], 1)
            own.then(nc.vector.tensor_copy(work[0:E, :], ps[0:E, 1, :]))
            for _ in range(SLOTS // 8):
                own.then(nc.vector.max(top[0:E, :], work[0:E, :]))
                own.then(nc.vector.match_replace(out=work[0:E, :], in_to_replace=top[0:E, :], in_values=work[0:E, :], imm_value=-1.0))
            nc.vector.tensor_scalar(work[0:E, :], work[0:E, :], -1.0, None, ALU.is_equal).then_inc(S["mask_done"], 1)
            dve.wait_ge(S["mask_turned"], 1)
            nc.vector.tensor_copy(taken[:, :, :].rearrange("p m e -> p (m e)"), ps[:, 2, 0:tiles * E]).then_inc(S["mask_back"], 1)
            dve.wait_ge(S["mask_back"], 1)
            dve.wait_ge(S["ranked"], 1)
            flat = slot[:, :, :].rearrange("p m e -> p (m e)")
            own.then(nc.vector.tensor_tensor(flat, ps[:, 3, 0:tiles * E], taken[:, :, :].rearrange("p m e -> p (m e)"), ALU.mult))
            own.then(nc.vector.tensor_scalar(flat, flat, -1.0, None, ALU.add))
            for m in range(tiles):
                by_slot = pick[:, m, :].rearrange("p (e s) -> p e s", e=E)
                own.then(nc.vector.tensor_tensor(by_slot, slot_iota[:, 0:SLOTS].unsqueeze(1).broadcast_to([P, E, SLOTS]),
                                                 slot[:, m, :].unsqueeze(2).broadcast_to([P, E, SLOTS]), ALU.is_equal))
                if m >= 2:
                    dve.wait_ge(S["pick_turned"], 2 * (m - 1))
                nc.vector.tensor_tensor(gated[:, m % 2, :].rearrange("p (e s) -> p e s", e=E), by_slot,
                                        aff[:, m, :].unsqueeze(2).broadcast_to([P, E, SLOTS]), ALU.mult).then_inc(S["gated_done"], 1)
                take(dve, nc.vector.tensor_copy, 2 * m, S["pick_even"])


def gather(nc, tag, x_hat, pick, gain, mod, xeT):
    tiles = TILES - CTX_TILES
    n_slots = EXPERTS * SLOTS
    with (
        nc.sbuf_tensor(f"{tag}_cols", [P, 3, KD], F32) as cols,
        nc.sbuf_tensor(f"{tag}_mul", [P, KD], F32) as mul,
        nc.psum_tensor(f"{tag}_ps", [P, 4, 512], F32) as ps,
        phase(nc, tag, "cols_in", "mul_done", "mm_done", "taken") as (block, S),
    ):
        jobs = [(k, half) for k in range(KD) for half in range(n_slots // 512)]

        @block.sync
        def _(sp):
            sp.dma_start(cols[:, 0, :], column(gain)).then_inc(S["cols_in"], 16)
            sp.dma_start(cols[:, 1, :], column(mod[0, 4 * D:5 * D])).then_inc(S["cols_in"], 16)
            sp.dma_start(cols[:, 2, :], column(mod[0, 3 * D:4 * D])).then_inc(S["cols_in"], 16)

        @block.tensor
        def _(pe):
            for n, (k, half) in enumerate(jobs):
                if n >= 4:
                    pe.wait_ge(S["taken"], n - 3)
                for m in range(tiles):
                    mm = nc.tensor.matmul(ps[:, n % 4, :], x_hat[:, CTX_TILES + m, k::KD], pick[:, m, half * 512:(half + 1) * 512],
                                          start=m == 0, stop=m == tiles - 1)
                mm.then_inc(S["mm_done"], 1)

        @block.vector
        def _(dve):
            dve.wait_ge(S["cols_in"], 48)
            nc.vector.scalar_tensor_tensor(mul[:, :], cols[:, 1, :], 1.0, cols[:, 0, :], ALU.add, ALU.mult).then_inc(S["mul_done"], 1)

        @block.scalar
        def _(act):
            act.wait_ge(S["mul_done"], 1)
            for n, (k, half) in enumerate(jobs):
                act.wait_ge(S["mm_done"], n + 1)
                nc.scalar.activation(xeT[:, k, half * 512:(half + 1) * 512], ps[:, n % 4, :], ACT.Identity,
                                     scale=mul[:, k:k + 1], bias=cols[:, 2, k:k + 1]).then_inc(S["taken"], 1)


def experts(nc, tag, xeT, w_gate, w_up, w_down, ident, ye, hid):
    F, FT = EXPERT_FF, EXPERT_FF // P
    cuts = [(a, min(a + 512, F)) for a in range(0, F, 512)]
    rows = [(a, min(a + 2, FT)) for a in range(0, FT, 2)]
    pieces = 2 * (KD + len(rows))
    RING = 7
    assert pieces % RING == 0 and 2 * SLOTS == P
    rounds = pieces // RING
    t_jobs = [(0, 4), (4, 8), (8, 11)]
    with contextlib.ExitStack() as stack:
        def sb(name, *shape):
            return stack.enter_context(nc.sbuf_tensor(f"{tag}_{name}", [P, *shape], F32))

        ring = sb("ring", RING, 2 * F)
        xs = sb("xs", KD, P)
        hidT = sb("hidT", FT, P)
        ps = stack.enter_context(nc.psum_tensor(f"{tag}_ps", [P, 8, 512], F32))
        block, S = stack.enter_context(phase(nc, tag, f"piece_in*{RING}", "piece_used", "slots_copied", "up_mm", "silu_done", "hid_done", "turned", "hid_turned",
                                             "down_mm", "out_done"))

        def pairs_of(eng):
            with eng.Fori(0, EXPERTS // 4) as i:
                for s in range(2):
                    yield 2 * i + s, i, s

        @block.sync
        def _(sp):
            with sp.Fori(0, EXPERTS // 2) as pair:
                for q in range(pieces):
                    j, side = divmod(q, 2)
                    e = 2 * pair + side
                    slot = q % RING
                    sp.wait_ge(S["piece_used"], pair * pieces + q + 1)
                    if j < KD:
                        for n, w in enumerate((w_gate, w_up)):
                            src = w[bass.ds(e, 1)].rearrange("a (p k) f -> p k (a f)", p=P)[:, j, :]
                            sp.dma_start(ring[:, slot, n * F:(n + 1) * F], src).then_inc(S["piece_in"][slot], 16)
                    else:
                        a, b = rows[j - KD]
                        src = w_down[bass.ds(e, 1)].rearrange("a (f p) d -> p (a f) d", p=P)
                        width = (b - a) * D // 2
                        for n in range(2):
                            part = src[:, a + n, :] if b - a == 2 else src[:, a, n * width:(n + 1) * width]
                            sp.dma_start(ring[:, slot, n * width:(n + 1) * width], part).then_inc(S["piece_in"][slot], 16)

        @block.gpsimd
        def _(pool):
            pool.sem_inc(S["slots_copied"], 1)
            for pair, i, s in pairs_of(pool):
                pool.wait_ge(S["up_mm"], pair + 2)
                nc.gpsimd.tensor_copy(xs[:, :, :], xeT[:, :, bass.ds(pair * P, P)]).then_inc(S["slots_copied"], 1)

        @block.tensor
        def _(pe):
            pe.sem_inc(S["piece_used"], RING)
            pe.sem_inc(S["up_mm"], 2)
            pe.sem_inc(S["turned"], 1)

            for pair, i, s in pairs_of(pe):
                def arrive(j):
                    for q in (2 * j, 2 * j + 1):
                        pe.wait_ge(S["piece_in"][q % RING], (pair * rounds + q // RING + 1) * 32)

                pe.wait_ge(S["slots_copied"], pair + 2)
                pe.wait_ge(S["hid_done"], pair + 1)
                for j in range(KD):
                    arrive(j)
                    for m in range(2 * len(cuts)):
                        for side in range(2):
                            n, c = divmod((m + 3 * side) % 6, 3)
                            a, b = cuts[c]
                            rows_of = slice(SLOTS * side, SLOTS * (side + 1))
                            mm = nc.tensor.matmul(ps[rows_of, 3 * n + c, 0:b - a], xs[:, j, rows_of], ring[:, (2 * j + side) % RING, n * F + a:n * F + b],
                                                  start=j == 0, stop=j == KD - 1)
                            if j < KD - 1 and m == 2 * len(cuts) - 1:
                                mm.then_inc(S["piece_used"], 1)
                            elif j == KD - 1 and m == 2 * len(cuts) - 1 and side == 1:
                                mm.then_inc(S["up_mm"], 1)
                pe.wait_ge(S["up_mm"], pair + 3)
                pe.sem_inc(S["piece_used"], 2)
                pe.wait_ge(S["hid_done"], pair + 2)
                pe.wait_ge(S["out_done"], pair + 1)
                for n, (a, b) in enumerate(t_jobs):
                    if n == 2:
                        pe.wait_ge(S["hid_turned"], 3 * pair + 1)
                    for f in range(a, b):
                        mm = nc.tensor.transpose(ps[:, 6 + n % 2, (f - a) * P:(f - a + 1) * P], hid[:, f * P:(f + 1) * P], ident)
                    mm.then_inc(S["turned"], 1)
                pe.wait_ge(S["hid_turned"], 3 * pair + 3)
                for j in range(KD, pieces // 2):
                    arrive(j)
                    a, b = rows[j - KD]
                    for f in range(a, b):
                        for m in range(2):
                            for side in range(2):
                                half = m ^ side
                                rows_of = slice(SLOTS * side, SLOTS * (side + 1))
                                at = (f - a) * D + half * 512
                                mm = nc.tensor.matmul(ps[rows_of, 6 + half, :], hidT[:, f, rows_of], ring[:, (2 * j + side) % RING, at:at + 512],
                                                      start=f == 0, stop=f == FT - 1)
                                if m == 1 and f == b - 1 and f < FT - 1:
                                    mm.then_inc(S["piece_used"], 1)
                mm.then_inc(S["down_mm"], 1)
                pe.wait_ge(S["down_mm"], pair + 1)
                pe.sem_inc(S["piece_used"], 2)

        @block.scalar
        def _(act):
            for pair, i, s in pairs_of(act):
                act.wait_ge(S["up_mm"], pair + 3)
                act.wait_ge(S["turned"], 3 * pair + 1)
                for c, (a, b) in enumerate(cuts):
                    nc.scalar.activation(hid[:, a:b], ps[:, c, 0:b - a], ACT.Silu).then_inc(S["silu_done"], 1)

        @block.vector
        def _(dve):
            dve.sem_inc(S["hid_done"], 1)
            dve.sem_inc(S["out_done"], 1)
            for pair, i, s in pairs_of(dve):
                for c, (a, b) in enumerate(cuts):
                    dve.wait_ge(S["silu_done"], 3 * pair + c + 1)
                    mul = nc.vector.tensor_tensor(hid[:, a:b], hid[:, a:b], ps[:, 3 + c, 0:b - a], ALU.mult)
                mul.then_inc(S["hid_done"], 1)
                for n, (a, b) in enumerate(t_jobs):
                    dve.wait_ge(S["turned"], 3 * pair + n + 2)
                    nc.vector.tensor_copy(hidT[:, a:b, :].rearrange("p f s -> p (f s)"), ps[:, 6 + n % 2, 0:(b - a) * P]).then_inc(S["hid_turned"], 1)
                dve.wait_ge(S["down_mm"], pair + 1)
                dst = ye[:, :, :].rearrange("p j d -> p (j d)")[:, bass.ds(pair * D, D)]
                nc.vector.tensor_copy(dst.rearrange("p (h d) -> p h d", h=2), ps[:, 6:8, :]).then_inc(S["out_done"], 1)


def scatter(nc, tag, pick_gateT, ye, y):
    tiles = TILES - CTX_TILES
    pairs = EXPERTS // 2
    with (
        nc.psum_tensor(f"{tag}_ps", [P, 4, 512], F32) as ps,
        phase(nc, tag, "mm_done", "taken_even", "taken_odd") as (block, S),
    ):
        jobs = [(m, half) for m in range(tiles) for half in range(2)]

        @block.tensor
        def _(pe):
            for n, (m, half) in enumerate(jobs):
                if n >= 4:
                    pe.wait_ge(S["taken_even"] if n % 2 == 0 else S["taken_odd"], (n - 4) // 2 + 1)
                for j in range(pairs):
                    mm = nc.tensor.matmul(ps[:, n % 4, :], pick_gateT[:, j, m * P:(m + 1) * P], ye[:, j, half * 512:(half + 1) * 512],
                                          start=j == 0, stop=j == pairs - 1)
                mm.then_inc(S["mm_done"], 1)

        def take(eng, copy, parity, done):
            for n, (m, half) in enumerate(jobs):
                if n % 2 == parity:
                    eng.wait_ge(S["mm_done"], n + 1)
                    copy(y[:, m, half * 512:(half + 1) * 512], ps[:, n % 4, :]).then_inc(done, 1)

        @block.vector
        def _(dve):
            take(dve, nc.vector.tensor_copy, 0, S["taken_even"])

        @block.scalar
        def _(act):
            take(act, nc.scalar.copy, 1, S["taken_odd"])


def second_block(nc, I, x, hT, mix, cst, ident, mod):
    conv_out = nc.dram_tensor("conv_out", (N_TOK, QKV), F32).ap()
    proj = nc.dram_tensor("proj2", (N_TOK, S_ALL), F32).ap()
    dn_q, dn_k = (nc.dram_tensor(f"dn_{n}", (N_TOK, D), F32).ap() for n in "qk")
    decay, beta = (nc.dram_tensor(f"dn_{n}", (N_TOK, 2 * DN_HEADS), F32).ap() for n in ("decay", "beta"))
    up_q, mla_q, mla_k = (nc.dram_tensor(n, (N_TOK, MLA_HEADS * MLA_DH), F32).ap() for n in ("up_q", "mla_q", "mla_k"))
    kv = nc.dram_tensor("mla_kv", (N_TOK, MLA_HEADS * (NOPE + MLA_DV)), F32).ap()
    lat = TILES - CTX_TILES
    modulation(nc, "moda", I["c_2"][0], I["c_ctx_2"], I["ada_w_2"][0], I["ada_b_2"][0], mod)
    load_tiles(nc, "ctx2", (x[:, 0:CTX_TILES, :], I["ctx_2"][0].rearrange("(m p) d -> p m d", p=P)))
    modulated_norm(nc, "n2", x, hT, ident, I["norm1_g_2"][0], mod, 0, 1)
    w_in = I["w_in_2"][0]
    conv_projection(nc, "conv", hT, w_in[:, 0:QKV], I["conv_w_2"][0], conv_out, ident)
    linear(nc, "in2", hT, KD, w_in[:, QKV:], TILES, out=proj)

    with nc.sbuf_tensor("cT", [P, Q_RANK // P, N_TOK], F32) as cT:
        latent_norm(nc, "cq", proj[:, S_CQ:S_CKV], I["q_a_norm_g_2"][0], cT, ident, CTX_TILES)
        linear(nc, "upq", cT, Q_RANK // P, I["w_uq_2"][0], lat, CTX_TILES, out=up_q)
        latent_norm(nc, "ckv", proj[:, S_CKV:S_KROPE], I["kv_a_norm_g_2"][0], cT, ident)
        linear(nc, "upkv", cT, KV_RANK // P, I["w_ukv_2"][0], TILES, out=kv)
    head_prep(nc, "qprep", [(0, MLA_DH, lambda r: up_q[r, :].rearrange("p (h f) -> p h f", h=MLA_HEADS))],
              I["q_norm_g_2"][0], I["rope_quarters"], mla_q, CTX_TILES)
    head_prep(nc, "kprep", [(0, NOPE, lambda r: kv[r, :].rearrange("p (h f) -> p h f", h=MLA_HEADS)[:, :, 0:NOPE]),
                            (NOPE, MLA_DH, lambda r: proj[r, S_KROPE:S_GATE].unsqueeze(1).broadcast_to([P, MLA_HEADS, ROPE]))],
              I["k_norm_g_2"][0], I["rope_quarters"], mla_k)
    attention(nc, "att2", mla_q, mla_k, kv, mix, 0, ident, MLA_HEADS, 1, MLA_DH, MLA_DV, NOPE + MLA_DV, NOPE, CTX_TILES)
    turn_over(nc, "tb", mix, hT, ident, CTX_TILES)
    with nc.sbuf_tensor("branch_b", [P, lat, D], F32) as b_out:
        linear(nc, "outb", hT, KD, I["w_out_b_2"][0], lat, CTX_TILES, out_sb=b_out)
        delta_prep(nc, "dprep", conv_out, proj, I["a_log_2"][0], I["dt_bias_2"][0], dn_q, dn_k, decay, beta)
        delta_scan(nc, "dn", DN_HEADS // 4, dn_q, dn_k, conv_out[:, 2 * D:], decay, beta, mix, cst)
        gated_readout(nc, "ro2", mix, DN_HEADS, proj, S_Z, I["dn_norm_g_2"][0], CTX_TILES)
        turn_over(nc, "ta", mix, hT, ident, CTX_TILES)
        linear(nc, "outa", hT, KD, I["w_out_a_2"][0], lat, CTX_TILES, out_sb=mix)
        merge(nc, "merge", mix, b_out, proj, S_GATE)
    turn_over(nc, "tm", mix, hT, ident, CTX_TILES, 0)
    linear(nc, "wo", hT, KD, I["w_o_2"][0], lat, CTX_TILES, out_sb=mix)
    gated_residual(nc, "resm", x, mix, mod, 2, None, CTX_TILES)


def mixture(nc, I, out, x, room, hT, mix, cst, ident, mod):
    n_slots = EXPERTS * SLOTS
    lat = TILES - CTX_TILES
    x_hat = mix
    modulated_norm(nc, "nm", x, hT, ident, I["norm2_g_2"][0], mod, 3, 4, CTX_TILES, x_hat=x_hat)
    with contextlib.ExitStack() as stack:
        def sb(name, *shape):
            return stack.enter_context(nc.sbuf_tensor(name, [P, *shape], F32))

        pick_gateT = sb("pick_gateT", n_slots // P, LAT)
        xeT = sb("xeT", KD, n_slots)
        with contextlib.ExitStack() as inner:
            pick = inner.enter_context(nc.sbuf_tensor("pick", [P, lat, n_slots], F32))
            ones = inner.enter_context(nc.sbuf_tensor("ones_sb", [P, P], F32))
            iota = inner.enter_context(nc.sbuf_tensor("slot_iota_sb", [P, SLOTS], F32))
            load_tiles(nc, "iota", (ones[:, :], I["ones"]), (iota[:, :], I["slot_numbers"]))
            route(nc, "route", hT, I["router_w_2"][0], cst, ones[:, :], iota, pick, pick_gateT)
            gather(nc, "gather", x_hat, pick, I["norm2_g_2"][0], mod, xeT)
        ye = room[:, 0:n_slots // P * D].rearrange("p (j d) -> p j d", d=D)
        y = room[:, n_slots // P * D:].rearrange("p (m d) -> p m d", d=D)
        hid = x[:, 0:CTX_TILES, :].rearrange("p m d -> p (m d)")[:, 0:EXPERT_FF]
        experts(nc, "experts", xeT, I["w_gate_2"][0], I["w_up_2"][0], I["w_down_2"][0], ident, ye, hid)
        scatter(nc, "scatter", pick_gateT, ye, y)
    gated_residual(nc, "resx", x, y, mod, 5, None, CTX_TILES)
    with phase(nc, "finish", "stored") as (block, S):
        @block.sync
        def _(sp):
            sp.dma_start(out[0].rearrange("(m p) d -> p m d", p=P), x[:, CTX_TILES:, :]).then_inc(S["stored"], 16)
            sp.wait_ge(S["stored"], 16)


def program(nc, I, out, first=True):
    mod2 = nc.dram_tensor("mod2", (2, 6 * D), F32).ap()
    with (
        nc.sbuf_tensor("x_sb", [P, TILES, D], F32) as x,
        nc.sbuf_tensor("room", [P, 2 * TILES * D], F32) as room,
    ):
        hT = room[:, 0:TILES * D].rearrange("p (k t) -> p k t", k=KD)
        mix = room[:, TILES * D:].rearrange("p (m d) -> p m d", d=D)
        with nc.sbuf_tensor("cst", [P, N_TABLES, P], F32) as cst:
            if first:
                first_block(nc, I, x, hT, mix, cst, cst[:, IDENT, :])
            else:
                load_tiles(nc, "start", (cst[:, :, :], I["tables"]), (x[:, CTX_TILES:, :], I["x"][0].rearrange("(m p) d -> p m d", p=P)))
            second_block(nc, I, x, hT, mix, cst, cst[:, IDENT, :], mod2)
        with nc.sbuf_tensor("cst_small", [P, 2, P], F32) as cst:
            load_tiles(nc, "small", (cst[:, :, :], I["tables"][:, 0:2, :]))
            mixture(nc, I, out, x, room, hT, mix, cst, cst[:, IDENT, :], mod2)


INPUTS = (
    "x", "c", "ctx", "c_ctx", "mod_w", "mod_b", "norm_pre_mix", "norm_post_mix", "norm_pre_ffn", "norm_post_ffn",
    "even_w_in", "gla_w_gate", "gla_b_gate", "gla_out_norm", "att_q_norm", "att_k_norm", "even_w_out",
    "odd_w_in", "hgrn_lower_bounds", "hgrn_out_norm", "odd_w_out", "ffn_w_gate", "ffn_w_up", "ffn_w_down",
    "c_2", "ctx_2", "c_ctx_2", "ada_w_2", "ada_b_2", "norm1_g_2", "norm2_g_2", "w_in_2", "conv_w_2", "a_log_2",
    "dt_bias_2", "dn_norm_g_2", "w_out_a_2", "q_a_norm_g_2", "w_uq_2", "kv_a_norm_g_2", "w_ukv_2", "q_norm_g_2",
    "k_norm_g_2", "w_out_b_2", "w_o_2", "router_w_2", "w_gate_2", "w_up_2", "w_down_2",
)


def kernel(**inputs):
    import numpy as np
    from concourse import bacc
    from concourse.bass_utils import run_bass_kernel_spmd

    nc = bacc.Bacc("TRN2", target_bir_lowering=False, num_devices=1)
    arrays = {name: np.ascontiguousarray(inputs[name]) for name in INPUTS}
    arrays["tables"] = tables()
    arrays["rope_pairs"] = rope_pairs()
    arrays["rope_quarters"] = rope_quarters()
    arrays["ones"] = np.ones((P, P), np.float32)
    arrays["slot_numbers"] = np.tile(np.arange(SLOTS, dtype=np.float32), (P, 1))
    arrays = {f"in_{name}": a for name, a in arrays.items()}
    aps = {name[3:]: nc.dram_tensor(name, a.shape, mybir.dt.from_np(a.dtype), kind="ExternalInput").ap() for name, a in arrays.items()}
    out = nc.dram_tensor("out", (1, LAT, D), F32, kind="ExternalOutput").ap()
    program(nc, aps, out)
    return run_bass_kernel_spmd(nc, [arrays], core_ids=[0]).results[0]["out"]
```
